# Optimizing a Trainium2 kernel written in Bass

```python
import jax, jax.numpy as jnp
from jax import lax
import numpy as np

D_MODEL = 1024
BATCH = 1
SEQ = 256
DEPTH = 1

CHUNK = 64
ATTN_HEADS = 8
ATTN_KV_HEADS = 2
HEAD_DIM = 64
ATTN_WIDTH = ATTN_HEADS * HEAD_DIM
KV_WIDTH = ATTN_KV_HEADS * HEAD_DIM
ATTN_SCALE = HEAD_DIM ** -0.5
IDX_HEADS = 4
IDX_DIM = 64
IDX_ROPE_DIM = 32
IDX_SCALE = (IDX_HEADS ** -0.5) * (IDX_DIM ** -0.5)
IDX_TOPK_MAX = 256
QUERY_BLOCK = 128
POOL_GROUPS = 4
POOL_WINDOWS = (2, 4, 8, 16)
POOL_WIDTH = 512
POOL_GROUP_DIM = POOL_WIDTH // POOL_GROUPS
N_EXPERTS = 32
TOP_K = 4
EXPERT_DIM = D_MODEL
SWIGLU_ALPHA = 1.702
SWIGLU_LIMIT = 7.0
EXPERT_BLOCK = 256
ROPE_THETA = 10000.0
NORM_EPS = 1e-6
IN_SPLITS = (ATTN_WIDTH, KV_WIDTH, KV_WIDTH, IDX_HEADS * IDX_DIM, IDX_DIM, IDX_HEADS, POOL_WIDTH, D_MODEL, D_MODEL)
IN_WIDTH = ATTN_WIDTH + 2 * KV_WIDTH + IDX_HEADS * IDX_DIM + IDX_DIM + IDX_HEADS + POOL_WIDTH + 2 * D_MODEL

kernel_name = "hybrid_dsa_pool_moe_block"

def rms_norm(x, g):
    xf = x.astype(jnp.float32)
    y = xf * lax.rsqrt(jnp.mean(xf * xf, axis=-1, keepdims=True) + NORM_EPS)
    return (y * g.astype(jnp.float32)).astype(x.dtype)

def layer_norm(x, g, b):
    xf = x.astype(jnp.float32)
    mu = jnp.mean(xf, axis=-1, keepdims=True)
    var = jnp.mean(jnp.square(xf - mu), axis=-1, keepdims=True)
    y = (xf - mu) * lax.rsqrt(var + NORM_EPS)
    return (y * g.astype(jnp.float32) + b.astype(jnp.float32)).astype(x.dtype)

def rope(x, positions):
    d = x.shape[-1]
    inv_freq = ROPE_THETA ** (-jnp.arange(0, d, 2, dtype=jnp.float32) / d)
    ang = positions.astype(jnp.float32)[:, :, None, None] * inv_freq
    cos, sin = jnp.cos(ang), jnp.sin(ang)
    xf = x.astype(jnp.float32)
    x1, x2 = xf[..., : d // 2], xf[..., d // 2:]
    return jnp.concatenate([x1 * cos - x2 * sin, x2 * cos + x1 * sin], axis=-1).astype(x.dtype)

def dsa_attention(q, k, v, q_idx, k_idx, w_idx):
    b, s = q.shape[0], q.shape[1]
    n_sel = min(IDX_TOPK_MAX, s // 4)
    n_blocks = s // QUERY_BLOCK
    groups = ATTN_HEADS // ATTN_KV_HEADS
    key_pos = jnp.arange(s, dtype=jnp.int32)
    k_idx_f = k_idx.astype(jnp.float32)

    def to_blocks(a):
        return jnp.moveaxis(a.reshape((b, n_blocks, QUERY_BLOCK) + a.shape[2:]), 1, 0)

    q_b = to_blocks(q.reshape(b, s, ATTN_KV_HEADS, groups, HEAD_DIM))
    qi_b = to_blocks(q_idx)
    w_b = to_blocks(w_idx)
    starts = jnp.arange(n_blocks, dtype=jnp.int32) * QUERY_BLOCK

    def block_fn(args):
        qb, qib, wb, t0 = args
        t = t0 + jnp.arange(QUERY_BLOCK, dtype=jnp.int32)
        chunk_end = (t // CHUNK + 1) * CHUNK
        logits = jnp.einsum('bthd,bsd->bths', qib.astype(jnp.float32), k_idx_f)
        score = jnp.einsum('bths,bth->bts', jax.nn.relu(logits), wb.astype(jnp.float32)) * IDX_SCALE
        admissible = key_pos[None, :] < chunk_end[:, None]
        score = jnp.where(admissible[None], score, -jnp.inf)
        _, sel = lax.top_k(score, n_sel)
        valid = sel < chunk_end[None, :, None]
        k_sel = jax.vmap(lambda kk, ii: kk[ii])(k, sel)
        v_sel = jax.vmap(lambda vv, ii: vv[ii])(v, sel)
        att = jnp.einsum('btrgd,btnrd->btrgn', qb.astype(jnp.float32), k_sel.astype(jnp.float32)) * ATTN_SCALE
        att = jnp.where(valid[:, :, None, None, :], att, -jnp.inf)
        prob = jax.nn.softmax(att, axis=-1)
        return jnp.einsum('btrgn,btnrd->btrgd', prob.astype(v.dtype), v_sel)

    out = lax.map(block_fn, (q_b, qi_b, w_b, starts))
    return jnp.moveaxis(out, 0, 1).reshape(b, s, ATTN_WIDTH)

def multiscale_pool(p, pool_mix_w, pool_scale):
    b, s, _ = p.shape
    pf = p.astype(jnp.float32).reshape(b, s, POOL_GROUPS, POOL_GROUP_DIM)
    csum = jnp.concatenate([jnp.zeros_like(pf[:, :1]), jnp.cumsum(pf, axis=1)], axis=1)
    t = jnp.arange(s, dtype=jnp.int32)
    means = []
    for g, w in enumerate(POOL_WINDOWS):
        lo = jnp.maximum(t + 1 - w, 0)
        cnt = jnp.minimum(t + 1, w).astype(jnp.float32)
        means.append((csum[:, 1:, g] - csum[:, lo, g]) / cnt[None, :, None])
    mean = jnp.stack(means, axis=2)
    mixed = (mean - pf).astype(p.dtype)
    mixed = jnp.einsum('bsgc,gcd->bsgd', mixed, pool_mix_w)
    return mixed.reshape(b, s, POOL_WIDTH) * pool_scale

def moe_ffn(h, router_w, router_b, w_gate_up, b_gate_up, w_down, b_down):
    b, s, d = h.shape
    n_tok = b * s
    hf = h.reshape(n_tok, d)
    logits = (hf @ router_w + router_b).astype(jnp.float32)
    top_vals, top_idx = lax.top_k(logits, TOP_K)
    gates = jax.nn.softmax(top_vals, axis=-1)
    n_assign = n_tok * TOP_K
    expert_flat = top_idx.reshape(-1)
    token_flat = jnp.arange(n_assign, dtype=jnp.int32) // TOP_K
    gate_flat = gates.reshape(-1)
    order = jnp.argsort(expert_flat)
    e_sorted = expert_flat[order]
    counts = jnp.bincount(expert_flat, length=N_EXPERTS)
    group_start = jnp.cumsum(counts) - counts
    padded = (counts + EXPERT_BLOCK - 1) // EXPERT_BLOCK * EXPERT_BLOCK
    pad_end = jnp.cumsum(padded)
    pad_start = pad_end - padded
    dest = pad_start[e_sorted] + (jnp.arange(n_assign, dtype=jnp.int32) - group_start[e_sorted])
    n_blocks = -(-(n_assign + N_EXPERTS * (EXPERT_BLOCK - 1)) // EXPERT_BLOCK)
    n_rows = n_blocks * EXPERT_BLOCK
    slot_token = jnp.full((n_rows,), n_tok, jnp.int32).at[dest].set(token_flat[order])
    slot_gate = jnp.zeros((n_rows,), jnp.float32).at[dest].set(gate_flat[order])
    block_expert = jnp.minimum(
        jnp.searchsorted(pad_end, jnp.arange(n_blocks, dtype=jnp.int32) * EXPERT_BLOCK, side='right'),
        N_EXPERTS - 1)
    h_pad = jnp.concatenate([hf, jnp.zeros((1, d), hf.dtype)], axis=0)

    def run_block(args):
        tok, e = args
        xb = h_pad[tok]
        gu = xb @ w_gate_up[e] + b_gate_up[e]
        gate = jnp.minimum(gu[:, :EXPERT_DIM], SWIGLU_LIMIT)
        up = jnp.clip(gu[:, EXPERT_DIM:], -SWIGLU_LIMIT, SWIGLU_LIMIT)
        act = gate * jax.nn.sigmoid(SWIGLU_ALPHA * gate) * (up + 1.0)
        return act @ w_down[e] + b_down[e]

    out = lax.map(run_block, (slot_token.reshape(n_blocks, EXPERT_BLOCK), block_expert))
    out = out.reshape(n_rows, d) * slot_gate[:, None].astype(out.dtype)
    y = jax.ops.segment_sum(out, slot_token, num_segments=n_tok + 1)[:n_tok]
    return y.reshape(b, s, d)

def setup_inputs(seed: int = 0) -> dict:
    key = jax.random.key(seed)
    ks = jax.random.split(key, 24)
    L = DEPTH

    def normal(k, shape, scale):
        return jax.random.normal(k, shape, jnp.float32) * scale

    x = normal(ks[0], (BATCH, SEQ, D_MODEL), 1.0)
    offsets = jax.random.randint(ks[1], (BATCH, 1), 0, 16, dtype=jnp.int32) * CHUNK
    positions = jnp.arange(SEQ, dtype=jnp.int32)[None, :] + offsets
    return {
        "x": x,
        "positions": positions,
        "norm1_g": 1.0 + normal(ks[2], (L, D_MODEL), 0.05),
        "w_in": normal(ks[3], (L, D_MODEL, IN_WIDTH), D_MODEL ** -0.5),
        "q_norm_g": 1.0 + normal(ks[4], (L, HEAD_DIM), 0.05),
        "k_norm_g": 1.0 + normal(ks[5], (L, HEAD_DIM), 0.05),
        "idx_k_norm_g": 1.0 + normal(ks[6], (L, IDX_DIM), 0.05),
        "idx_k_norm_b": normal(ks[7], (L, IDX_DIM), 0.05),
        "w_branch_attn": normal(ks[8], (L, ATTN_WIDTH, D_MODEL), ATTN_WIDTH ** -0.5),
        "pool_mix_w": normal(ks[9], (L, POOL_GROUPS, POOL_GROUP_DIM, POOL_GROUP_DIM), POOL_GROUP_DIM ** -0.5),
        "pool_scale": 1.0 + normal(ks[10], (L, POOL_WIDTH), 0.05),
        "w_branch_pool": normal(ks[11], (L, POOL_WIDTH, D_MODEL), POOL_WIDTH ** -0.5),
        "w_out": normal(ks[12], (L, D_MODEL, D_MODEL), D_MODEL ** -0.5),
        "norm2_g": 1.0 + normal(ks[13], (L, D_MODEL), 0.05),
        "router_w": normal(ks[14], (L, D_MODEL, N_EXPERTS), D_MODEL ** -0.5),
        "router_b": normal(ks[15], (L, N_EXPERTS), 0.01),
        "w_gate_up": normal(ks[16], (L, N_EXPERTS, D_MODEL, 2 * EXPERT_DIM), D_MODEL ** -0.5),
        "b_gate_up": normal(ks[17], (L, N_EXPERTS, 2 * EXPERT_DIM), 0.02),
        "w_down": normal(ks[18], (L, N_EXPERTS, EXPERT_DIM, D_MODEL), EXPERT_DIM ** -0.5),
        "b_down": normal(ks[19], (L, N_EXPERTS, D_MODEL), 0.02),
    }

def reference(x, positions, norm1_g, w_in, q_norm_g, k_norm_g, idx_k_norm_g, idx_k_norm_b,
              w_branch_attn, pool_mix_w, pool_scale, w_branch_pool, w_out, norm2_g,
              router_w, router_b, w_gate_up, b_gate_up, w_down, b_down):
    b, s, _ = x.shape
    split_at = np.cumsum(IN_SPLITS)[:-1].tolist()
    for l in range(DEPTH):
        h = rms_norm(x, norm1_g[l])
        proj = h @ w_in[l]
        q, k, v, qi, ki, wi, pool_in, gate_a, gate_p = jnp.split(proj, split_at, axis=-1)
        q = rope(rms_norm(q.reshape(b, s, ATTN_HEADS, HEAD_DIM), q_norm_g[l]), positions)
        k = rope(rms_norm(k.reshape(b, s, ATTN_KV_HEADS, HEAD_DIM), k_norm_g[l]), positions)
        v = v.reshape(b, s, ATTN_KV_HEADS, HEAD_DIM)
        qi = qi.reshape(b, s, IDX_HEADS, IDX_DIM)
        qi = jnp.concatenate([rope(qi[..., :IDX_ROPE_DIM], positions), qi[..., IDX_ROPE_DIM:]], axis=-1)
        ki = layer_norm(ki, idx_k_norm_g[l], idx_k_norm_b[l])[:, :, None, :]
        ki = jnp.concatenate([rope(ki[..., :IDX_ROPE_DIM], positions), ki[..., IDX_ROPE_DIM:]], axis=-1)[:, :, 0]
        attn = dsa_attention(q, k, v, qi, ki, wi)
        pooled = multiscale_pool(pool_in, pool_mix_w[l], pool_scale[l])
        merged = (jax.nn.sigmoid(gate_a) * (attn @ w_branch_attn[l])
                  + jax.nn.sigmoid(gate_p) * (pooled @ w_branch_pool[l]))
        x = x + merged @ w_out[l]
        h2 = rms_norm(x, norm2_g[l])
        x = x + moe_ffn(h2, router_w[l], router_b[l], w_gate_up[l], b_gate_up[l], w_down[l], b_down[l])
    return x


_drawn_inputs = setup_inputs


def setup_inputs(seed=0):
    import zlib

    import numpy as np

    out = dict(_drawn_inputs(seed))
    spreads = {}
    factors = {'q_norm_g': 2.762, 'b_gate_up': 5.549, 'b_down': 6.459}
    for name, (base, spread) in spreads.items():
        noise = np.random.default_rng([zlib.crc32(name.encode()), seed]).standard_normal(out[name].shape)
        drawn = base * np.exp(spread * noise) if base else spread * noise
        out[name] = __import__('jax').numpy.asarray(drawn.astype(out[name].dtype))
    for name, factor in factors.items():
        out[name] = (out[name] * factor).astype(out[name].dtype)
    return out
```

```python
import concourse.bass as bass
from concourse import mybir
from contextlib import ExitStack

P = 128
SEQ = 256
D = 1024
NB = SEQ // P
KC = D // P
HEADS, KV, HD = 8, 2, 64
IH, ID, IROPE = 4, 64, 32
CHUNK = 64
N_SEL = 64
GROUPS, PW = 4, 512
WINDOWS = (2, 4, 8, 16)
E, TOPK = 32, 4
T = 64
PAIRS = E // 2
BANK = 512
C_Q, C_K, C_QI, C_KI, C_POOL, C_GA, C_GP = 0, 512, 768, 1024, 1092, 1604, 2628
IN_W = 3652
EPS = 1e-6
SCALE = HD ** -0.5
IDX_SCALE = (IH ** -0.5) * (ID ** -0.5)
ALPHA, LIMIT = 1.702, 7.0

K_IDENT, K_TRI, K_ONES, K_IOTA, K_INVF = 0, 128, 256, 384, 448
K_W = 480
R_QG, R_KG, R_IG, R_IB, R_RB = 0, 64, 128, 192, 256
R_W = 288
P_G1, P_PS, P_G2 = 0, 8, 12
P_W = 20

SLOTS = 12
PRE_UNITS = 24
PAIR_UNITS = 24
UW = 2048

NEG_MASK = -3.0e38
REPL = -3.4e38
PAD = -3.39e38
BIG_RANK = 1.0e6
TWO_PI = 6.283185307179586
MAGIC = 12582912.0


def two_pi_parts():
    import numpy as np
    c1 = 6.28125
    c2 = float(np.float32(np.floor((TWO_PI - c1) * 2.0 ** 21) / 2.0 ** 21))
    c3 = float(np.float32(TWO_PI - c1 - c2))
    return c1, c2, c3


def block_kernel(nc, x_d, pos_d, w_in, w_a, w_b, w_out, mix_d, router_d, w_gu, w_dn, b_dn,
                 consts_d, bands_d, rows_d, cols_d, bgu_d, out_d):
    f32, i32 = mybir.dt.float32, mybir.dt.int32
    ALU = mybir.AluOpType
    ACT = mybir.ActivationFunctionType
    AX = mybir.AxisListType.X
    ctx = ExitStack()
    with ctx:
        def sb(name, width, dt=f32, parts=P):
            return ctx.enter_context(nc.sbuf_tensor(name, [parts, width], dt))

        def sem(name):
            return ctx.enter_context(nc.semaphore(name))

        def v3(ap, a):
            return ap.rearrange("p (a n) -> p a n", a=a)

        def v4(ap, a, b):
            return ap.rearrange("p (a b n) -> p a b n", a=a, b=b)

        ring = [sb(f"ring{s}", UW) for s in range(SLOTS)]
        consts = sb("consts", K_W)
        rows = sb("rows", R_W)
        cols = sb("cols", P_W)
        bgu_t = sb("bgu", E * KC * 2)
        small = sb("small", 256)
        x_t = sb("x", NB * D)
        xn_t = sb("xn", NB * D)
        hT_t = sb("hT", KC * SEQ)
        siga_t = sb("siga", NB * D)
        sigp_t = sb("sigp", NB * D)
        kvqi_t = sb("kvqi", NB * 512)
        kiwi_t = sb("kiwi", NB * 68)
        q_t = sb("q", NB * 512)
        pool_t = sb("pool", NB * 512)
        kdup_t = sb("kdup", NB * KV * P)
        kqT_t = sb("kqT", (KV + 2) * SEQ)
        kidup_t = sb("kidup", NB * P)
        kiT_t = sb("kiT", SEQ)
        qT_t = sb("qT", 4 * SEQ)
        rt_t = sb("rt", 2 * NB * SEQ)
        attnT_t = sb("attnT", 4 * SEQ)
        big = sb("big", 6144)
        mixw_t = sb("mixw", GROUPS * P)
        posi = sb("posi", NB, i32)
        n_t = sb("n_iter", 1, i32)
        selb, selgb, selgT = (kqT_t[:, 256 * j:256 * j + 256] for j in range(3))
        rank_t = sb("rank", NB * E)
        gat_t = sb("gates", NB * E)

        ident = consts[:, K_IDENT:K_IDENT + P]
        tri = consts[:, K_TRI:K_TRI + P]
        ones = consts[:, K_ONES:K_ONES + P]
        iota = consts[:, K_IOTA:K_IOTA + T]
        invf = consts[:, K_INVF:K_INVF + 32]
        x = v3(x_t[:, :], NB)
        xn = v3(xn_t[:, :], NB)
        hT = v3(hT_t[:, :], KC)
        siga, sigp = v3(siga_t[:, :], NB), v3(sigp_t[:, :], NB)
        kvqi, kiwi = v3(kvqi_t[:, :], NB), v3(kiwi_t[:, :], NB)
        qq, pool = v3(q_t[:, :], NB), v3(pool_t[:, :], NB)
        kdup = kdup_t[:, :].rearrange("p (b k c) -> p b k c", b=NB, k=KV)
        kT, qiT, qT = v3(kqT_t[:, 0:512], KV), v3(kqT_t[:, 512:1024], 2), v3(qT_t[:, :], 4)
        kidup = v3(kidup_t[:, :], NB)
        score, pen = v3(rt_t[:, 0:512], NB), v3(rt_t[:, 512:1024], NB)
        attnT = v3(attnT_t[:, :], 4)
        bands_t = big[:, 4096:5632]
        bands = v4(bands_t, GROUPS, 3)
        mixw = v3(mixw_t[:, :], GROUPS)
        relu = v3(big[:, 0:1024], 4)
        att = [v3(big[:, 0:1024], HEADS), v3(xn_t[:, :], HEADS)]
        PT = [big[:, 1024:2048].rearrange("p (k h q) -> p k h q", k=1, h=HEADS),
              big[:, 2048:4096].rearrange("p (k h q) -> p k h q", k=2, h=HEADS)]
        work = v3(big[:, 5632:6144], NB)
        mixedT, pooledT = v3(big[:, 0:1024], GROUPS), v3(big[:, 1024:2048], GROUPS)
        rtmp = [big[:, 1024 + 512 * j:1536 + 512 * j] for j in range(4)]
        angs = [big[:, 3072 + 64 * j:3136 + 64 * j] for j in range(6)]
        cos_t, sin_t = small[:, 0:64], small[:, 64:128]
        xg = big[:, 0:1024]
        xgT = v3(big[:, 1024:2048], KC)
        gu_sb = big[:, 2048:3072]
        gu1 = big[:, 3072:4096].rearrange("p (c g s) -> p c g s", c=KC, g=2)
        actT = v3(big[:, 4096:5120], KC)
        dsb = big[:, 5120:6144]
        sg = v3(kvqi_t[:, 0:512], KC)
        up1 = v3(kvqi_t[:, 512:1024], KC)
        sel = selb[:, :].rearrange("p (b e s) -> p b e s", b=NB, e=2)
        selg = selgb[:, :].rearrange("p (b e s) -> p b e s", b=NB, e=2)
        rank, gat = v3(rank_t[:, :], NB), v3(gat_t[:, :], NB)
        bgu = bgu_t[:, :].rearrange("p (e c g) -> p e c g", e=E, c=KC)
        bd_sb = q_t[0:E, :]
        rw = v3(pool_t[:, 0:KC * E], KC)

        bank = [ctx.enter_context(nc.psum_tensor(f"bank{j}", [P, BANK], f32)) for j in range(8)]
        PAIR_BANKS = [(0, 1), (2, 3), (4, 5)]
        TB = [bank[6], bank[7]]

        unit_in = [sem(f"unit_in{s}") for s in range(SLOTS)]
        unit_used = [sem(f"unit_used{s}") for s in range(SLOTS)]
        x_in = [sem("x_in0"), sem("x_in1")]
        ident_in, cols_in, small_in, late_in = sem("ident_in"), sem("cols_in"), sem("small_in"), sem("late_in")
        rw_in, bd_in = sem("rw_in"), sem("bd_in")
        act_step, dve_step = sem("act_step"), sem("dve_step")
        xn_ready = sem("xn_ready")
        t_ready = sem("t_ready")
        t_read = [sem("t_read0"), sem("t_read1")]
        job_ready, job_read = sem("job_ready"), sem("job_read")
        gate_out = sem("gate_out")
        ms_ready, root_ready = sem("ms_ready"), sem("root_ready")
        trig_arg, trig_ready = sem("trig_arg"), sem("trig_ready")
        roped = sem("roped")
        relu_ready, relu_used = sem("relu_ready"), sem("relu_used")
        mixedT_ready = sem("mixedT_ready")
        att_masked, att_exp, prob_ready = sem("att_masked"), sem("att_exp"), sem("prob_ready")
        merged_ready, x2_ready, h2_ready = sem("merged_ready"), sem("x2_ready"), sem("h2_ready")
        lg_ready, ex_ready, gates_ready = sem("lg_ready"), sem("ex_ready"), sem("gates_ready")
        n_ready = sem("n_ready")
        out_done = sem("out_done")
        sel_ready, selg_ready, rank_down = sem("sel_ready"), sem("selg_ready"), sem("rank_down")
        gu_done = [sem("guA_done"), sem("guB_done")]
        gu_copied = [sem("guA_copied"), sem("guB_copied")]
        biased, clipped = sem("biased"), sem("clipped")
        sig_ready, act_ready = sem("sig_ready"), sem("act_ready")
        up_ready, prod_ready = sem("up_ready"), sem("prod_ready")
        down_done = sem("down_done")
        d_copied = [sem("d_copied0"), sem("d_copied1")]
        JOBS = ["TA0", "TA1", "S0", "S1", "G0", "G1", "TB0", "TB1", "X0", "X1", "Y0", "Y1", "Y2", "Y3"]
        done = {j: sem(f"{j}_done") for j in JOBS}
        read = {j: sem(f"{j}_read") for j in JOBS}

        groups = [(C_K, 512), (C_KI, 68), (C_Q, 512), (C_POOL, 512),
                  (C_GA, 512), (C_GA + 512, 512), (C_GP, 512), (C_GP + 512, 512)]

        def pre_unit_src(u):
            if u < 16:
                c0, n = groups[u // 2]
                k0 = 4 * (u % 2)
                return w_in[k0 * P:(k0 + 4) * P, c0:c0 + n].rearrange("(k p) n -> p k n", p=P), n * 4
            w, r0 = [(w_a, 16), (w_b, 18), (w_out, 20)][0 if u < 18 else 1 if u < 20 else 2]
            r = (u - r0) * 2 * P
            return w[r:r + 2 * P, :].rearrange("(k p) n -> p k n", p=P), 2 * D

        def pair_unit_src(p, u):
            if u < 16:
                row = (2 * p + u // 8) * D + (u % 8) * P
                return w_gu[bass.ds(row, P), :]
            j = u - 16
            row = (2 * p + j % 2) * D + (j // 2) * 2 * P
            return w_dn[bass.ds(row, 2 * P), :].rearrange("(k p) n -> p k n", p=P)

        (TJ_X, TJ_K, TJ_QI, TJ_KI, TJ_L0, TJ_L1, TJ_Q, TJ_MIX, TJ_POOL, TJ_S0, TJ_S1,
         TJ_P0, TJ_P1, TJ_O, TJ_M, TJ_H2, TJ_R, TJ_RANK, TJ_G) = (
            0, 4, 5, 6, 7, 9, 11, 25, 29, 13, 15, 19, 21, 27, 31, 35, 39, 40, 41)
        BJ_WA, BJ_WB, BJ_WO, BJ_BD = 8, 10, 12, 14

        def short_read(eng, n):
            eng.wait_ge(t_read[0], (n + 1) // 2)
            eng.wait_ge(t_read[1], n // 2)

        block = ctx.enter_context(nc.Block())

        @block.sync
        def _(sp):
            for b in range(NB):
                sp.dma_start(x[:, b, :], x_d[b * P:(b + 1) * P, :]).then_inc(x_in[b], 16)

            def pre_unit(u):
                s = u % SLOTS
                if u >= SLOTS:
                    sp.wait_ge(unit_used[s], u // SLOTS)
                src, w = pre_unit_src(u)
                k = 4 if u < 16 else 2
                sp.dma_start(v3(ring[s][:, 0:w], k), src).then_inc(unit_in[s], 16)

            def pair_unit(p, u, uses):
                s = u % SLOTS
                sp.wait_ge(unit_used[s], uses)
                dst = ring[s][:, :] if u < 16 else v3(ring[s][:, :], 2)
                sp.dma_start(dst, pair_unit_src(p, u)).then_inc(unit_in[s], 16)

            for u in range(PRE_UNITS):
                pre_unit(u)
            for u in range(SLOTS):
                pair_unit(0, u, PRE_UNITS // SLOTS)
            sp.wait_ge(n_ready, 1)
            n = sp.value_load(n_t[0:1, 0:1], min_val=PAIRS, max_val=4 * PAIRS)
            with sp.Fori(0, n - 1) as it:
                here = sp.snap(it % PAIRS)
                after = sp.snap((it + 1) % PAIRS)
                uses1 = sp.snap(2 * it + 3)
                uses2 = sp.snap(2 * it + 4)
                for u in range(SLOTS, PAIR_UNITS):
                    pair_unit(here, u, uses1)
                for u in range(SLOTS):
                    pair_unit(after, u, uses2)
            last_uses = sp.snap(2 * n + 1)
            for u in range(SLOTS, PAIR_UNITS):
                pair_unit(PAIRS - 1, u, last_uses)
            credit = sp.snap(n + 1)
            for j in range(4):
                b, h = j // 2, j % 2
                sp.wait_ge(read[f"Y{j}"], credit)
                sp.dma_start(out_d[b * P:(b + 1) * P, 512 * h:512 * h + 512], x[:, b, 512 * h:512 * h + 512]).then_inc(out_done, 16)
            sp.wait_ge(out_done, 64)

        @block.gpsimd
        def _(pool_e):
            pool_e.dma_start(consts[:, P:K_W], consts_d[:, P:K_W]).then_inc(small_in, 16)
            pool_e.dma_start(rows[:, :], rows_d.to_broadcast([P, R_W])).then_inc(small_in, 16)
            pool_e.dma_start(posi[:, :], pos_d).then_inc(small_in, 16)
            pool_e.dma_start(bands_t, bands_d).then_inc(late_in, 16)
            pool_e.dma_start(mixw, mix_d.rearrange("g c d -> c g d")).then_inc(late_in, 16)
            pool_e.dma_start(bgu_t[:, :], bgu_d).then_inc(late_in, 16)
            pool_e.wait_ge(t_ready, TJ_Q + 2)
            pool_e.dma_start(q_t[0:E, :], b_dn).then_inc(bd_in, 16)
            pool_e.wait_ge(t_ready, TJ_MIX + 2)
            pool_e.dma_start(rw, router_d.rearrange("(k p) e -> p k e", p=P)).then_inc(rw_in, 16)

        @block.scalar
        def _(act):
            steps = [0]

            def step(ins):
                steps[0] += 1
                ins.then_inc(act_step, 1)
                act.wait_ge(act_step, steps[0])

            def evac(dst, src, s):
                return nc.scalar.activation(dst, src, ACT.Copy).then_inc(s, 1)

            def root(col, n, which):
                act.wait_ge(ms_ready, which)
                nc.scalar.activation(small[:, col:col + n], small[:, col:col + n], ACT.Sqrt).then_inc(root_ready, 1)

            for j in JOBS:
                if j.startswith("Y"):
                    act.sem_inc(read[j], 1)
            for s in (*gu_copied, *d_copied, act_ready):
                act.sem_inc(s, 1)
            act.dma_start(ident, consts_d[:, 0:P]).then_inc(ident_in, 16)
            act.dma_start(cols[:, :], cols_d).then_inc(cols_in, 16)
            for b in range(NB):
                act.wait_ge(x_in[b], 16)
                nc.scalar.activation(xn[:, b, :], x[:, b, :], ACT.Square, accum_out=small[:, 128 + b:129 + b]).then_inc(xn_ready, 1)
            root(128, 2, 1)
            act.wait_ge(trig_arg, 2)
            nc.scalar.activation(sin_t, angs[1], ACT.Sin).then_inc(trig_ready, 1)
            nc.scalar.activation(cos_t, angs[3], ACT.Sin).then_inc(trig_ready, 1)

            act.wait_ge(root_ready, 2)

            def job(j, dst):
                for b in range(NB):
                    act.wait_ge(job_ready, 2 * j + b + 1)
                    n = groups[j][1]
                    src = bank[PAIR_BANKS[j % 3][b]][:, 0:n]
                    nc.scalar.activation(dst[:, b, :], src, ACT.Copy, scale=small[:, 128 + b:129 + b]).then_inc(job_read, 1)

            def gate_job(j, dst, half):
                for b in range(NB):
                    act.wait_ge(job_ready, 2 * j + b + 1)
                    src = bank[PAIR_BANKS[j % 3][b]][:, :]
                    nc.scalar.activation(dst[:, b, half * 512:half * 512 + 512], src, ACT.Sigmoid,
                                         scale=small[:, 128 + b:129 + b]).then_inc(job_read, 1)

            def tcopy(j, dst, n=BANK, func=ACT.Copy):
                act.wait_ge(t_ready, j + 1)
                src = TB[j % 2][:, 0:n]
                if len(dst.shape) == 3:
                    src = v3(src, dst.shape[1])
                if len(dst.shape) == 4:
                    src = v4(src, dst.shape[1], dst.shape[2])
                nc.scalar.activation(dst, src, func).then_inc(t_read[j % 2], 1)

            job(0, kvqi)
            job(1, kiwi)
            root(132, 6, 2)
            job(2, qq)
            root(140, 16, 3)
            job(3, pool)
            tcopy(TJ_K, kT.rearrange("p k (b t) -> p b k t", b=NB))
            tcopy(TJ_QI, qiT.rearrange("p k (b t) -> p b k t", b=NB))
            tcopy(TJ_KI, kiT_t[:, :], SEQ)
            for par in range(2):
                tcopy(TJ_L0 + par, relu[:, par::2, 0:P], 2 * P, ACT.Relu)
            act.wait_ge(relu_used, 1)
            for par in range(2):
                tcopy(TJ_L1 + par, relu[:, par::2, :], BANK, ACT.Relu)
            gate_job(4, siga, 0)
            for b in range(NB):
                tcopy(TJ_Q + b, qT[:, :, b * P:b * P + P])
            gate_job(5, siga, 1)
            for b in range(NB):
                act.wait_ge(att_masked, b + 1)
                for h in range(HEADS):
                    nc.scalar.activation(att[b][:, h, :], att[b][:, h, :], ACT.Exp,
                                         bias=small[:, 156 + 8 * b + h:157 + 8 * b + h],
                                         accum_out=small[:, 172 + 8 * b + h:173 + 8 * b + h]).then_inc(att_exp, 1)
            gate_job(6, sigp, 0)
            tcopy(TJ_P0, PT[0][:, 0, 0:4, :])
            tcopy(TJ_P1, PT[1][:, 0, 0:4, :])
            tcopy(TJ_P1 + 2, PT[1][:, 1, 0:4, :])
            gate_job(7, sigp, 1)
            for j in range(2):
                tcopy(TJ_MIX + j, mixedT[:, 2 * j:2 * j + 2, :])
            for b in range(NB):
                tcopy(TJ_O + b, attnT[:, :, b * P:b * P + P])
            for j in (0, 2):
                tcopy(TJ_M + j, hT[:, 0:4, (j // 2) * P:(j // 2) * P + P])
            for b in range(NB):
                act.wait_ge(x2_ready, b + 1)
                nc.scalar.activation(xn[:, b, :], x[:, b, :], ACT.Square, accum_out=small[:, 128 + b:129 + b]).then_inc(xn_ready, 1)
            root(128, 2, 4)
            act.wait_ge(root_ready, 8)
            act.wait_ge(xn_ready, 2 * NB)
            for b in range(NB):
                nc.scalar.activation(xn[:, b, :], x[:, b, :], ACT.Copy, scale=small[:, 128 + b:129 + b]).then_inc(xn_ready, 1)
            act.wait_ge(lg_ready, 1)
            for b in range(NB):
                nc.scalar.activation(rt_t[:, 128 + 32 * b:160 + 32 * b], rt_t[:, 40 * b:40 * b + E], ACT.Exp,
                                     bias=small[:, 190 + b:191 + b]).then_inc(ex_ready, 1)
            act.wait_ge(t_ready, TJ_G + 1)
            nc.scalar.activation(rt_t[0:E, 256:256 + SEQ], TB[TJ_G % 2][0:E, 0:SEQ], ACT.Copy).then_inc(t_read[TJ_G % 2], 1)

            def take(j, dst, src, count):
                act.wait_ge(done[j], count)
                nc.scalar.activation(dst, src, ACT.Copy).then_inc(read[j], 1)

            def take_gather(count):
                for h in range(2):
                    take(f"G{h}", xg[:, h * 512:h * 512 + 512], TB[h][:, :], count)

            take_gather(1)
            act.wait_ge(n_ready, 1)
            n = act.value_load(n_t[0:1, 0:1], min_val=PAIRS, max_val=4 * PAIRS)
            with act.Fori(0, n) as it:
                c1 = act.snap(it + 1)
                c2 = act.snap(it + 2)
                c21 = act.snap(2 * it + 1)
                c22 = act.snap(2 * it + 2)

                def copy_gu(e, done_count):
                    act.wait_ge(gu_done[e], done_count)
                    for h in range(2):
                        ins = nc.scalar.activation(gu_sb[:, h * 512:h * 512 + 512], bank[2 * e + h][:, :], ACT.Copy)
                    ins.then_inc(gu_copied[e], 1)

                def sigmoid(count):
                    act.wait_ge(clipped, count)
                    nc.scalar.activation(sg, gu1[:, :, 0, :], ACT.Sigmoid, scale=ALPHA).then_inc(sig_ready, 1)

                copy_gu(0, c1)
                for h in range(2):
                    take(f"S{h}", selgT[:, h * P:h * P + P], TB[h][:, 0:P], c1)
                sigmoid(c21)
                copy_gu(1, c1)
                take_gather(c2)
                sigmoid(c22)
                act.wait_ge(down_done, c1)
                nc.scalar.activation(dsb[:, 0:512], bank[4][:, :], ACT.Copy).then_inc(d_copied[0], 1)

        @block.vector
        def _(dve):
            steps = [0]

            def step(ins):
                steps[0] += 1
                ins.then_inc(dve_step, 1)
                dve.wait_ge(dve_step, steps[0])

            V = nc.vector
            rdy = [0]

            def root_and_reciprocal(col, n, scale, which):
                V.tensor_scalar(small[:, col:col + n], small[:, col:col + n], scale, EPS, ALU.mult, ALU.add).then_inc(ms_ready, 1)
                dve.wait_ge(root_ready, 2 * which - 1)
                V.reciprocal(small[:, col:col + n], small[:, col:col + n]).then_inc(root_ready, 1)
                dve.wait_ge(root_ready, 2 * which)

            def gained(j, c0, b, gain):
                dve.wait_ge(t_ready, j + 1)
                g = cols[:, gain + c0:gain + c0 + 4].unsqueeze(2).to_broadcast([P, 4, P])
                V.tensor_tensor(hT[:, c0:c0 + 4, b * P:b * P + P], v3(TB[j % 2][:, :], 4), g, ALU.mult).then_inc(t_read[j % 2], 1)

            dve.wait_ge(cols_in, 16)
            for j in range(4):
                gained(TJ_X + j, 4 * (j % 2), j // 2, P_G1)
            dve.wait_ge(xn_ready, NB)
            root_and_reciprocal(128, 2, 1.0 / D, 1)
            dve.wait_ge(small_in, 48)
            posf = small[:, 188:190]
            step(V.tensor_copy(posf, posi[:, :]))
            for b in range(NB):
                step(V.tensor_scalar(angs[0][:, 32 * b:32 * b + 32], invf, posf[:, b:b + 1], None, ALU.mult))
            step(V.tensor_scalar(angs[2], angs[0], 1.0 / TWO_PI, None, ALU.mult))
            step(V.tensor_scalar(angs[4], angs[2], MAGIC, None, ALU.add))
            step(V.tensor_scalar(angs[2], angs[4], MAGIC, None, ALU.subtract))
            for part in two_pi_parts():
                step(V.scalar_tensor_tensor(out=angs[0], in0=angs[2], scalar=-part, in1=angs[0], op0=ALU.mult, op1=ALU.add))
            V.tensor_scalar(angs[1], angs[0], 3.1415925, -3.1415925, ALU.min, ALU.max).then_inc(trig_arg, 1)
            step(V.scalar_tensor_tensor(out=angs[4], in0=angs[0], scalar=-1.0, in1=angs[0], op0=ALU.mult, op1=ALU.max))
            V.tensor_scalar(angs[3], angs[4], -1.0, TWO_PI / 4, ALU.mult, ALU.add).then_inc(trig_arg, 1)

            cos = v3(cos_t, NB)
            sin = v3(sin_t, NB)

            def rope(src, outs, nh, half, stride):
                cb = cos[:, :, ::stride].unsqueeze(2).to_broadcast([P, NB, nh, half])
                sb_ = sin[:, :, ::stride].unsqueeze(2).to_broadcast([P, NB, nh, half])
                x1, x2 = src[:, :, :, 0:half], src[:, :, :, half:2 * half]
                t = [r[:, 0:NB * nh * half].rearrange("p (b h n) -> p b h n", b=NB, h=nh) for r in rtmp]
                V.tensor_tensor(t[0], x1, cb, ALU.mult)
                V.tensor_tensor(t[1], x2, sb_, ALU.mult)
                V.tensor_tensor(t[2], x2, cb, ALU.mult)
                step(V.tensor_tensor(t[3], x1, sb_, ALU.mult))
                for o in outs:
                    V.tensor_tensor(o[:, :, :, 0:half], t[0], t[1], ALU.subtract)
                    ins = V.tensor_tensor(o[:, :, :, half:2 * half], t[2], t[3], ALU.add)
                return ins

            def head_squares(src, nh, col):
                sq = big[:, 1024:1024 + NB * nh * HD].rearrange("p (b h n) -> p b h n", b=NB, h=nh)
                step(V.tensor_tensor(sq, src, src, ALU.mult))
                step(V.tensor_reduce(out=small[:, col:col + NB * nh], in_=big[:, 1024:1024 + NB * nh * HD].rearrange("p (a n) -> p a n", n=HD),
                                     op=ALU.add, axis=AX))

            def scaled(src, nh, col, gain):
                r = small[:, col:col + NB * nh].rearrange("p (b h) -> p b h", b=NB).unsqueeze(3).to_broadcast([P, NB, nh, HD])
                g = gain.unsqueeze(1).unsqueeze(1).to_broadcast([P, NB, nh, HD])
                step(V.tensor_tensor(src, src, r, ALU.mult))
                step(V.tensor_tensor(src, src, g, ALU.mult))

            k4 = kvqi[:, :, 0:128].rearrange("p b (h n) -> p b h n", h=KV)
            qi4 = kvqi[:, :, 256:512].rearrange("p b (h n) -> p b h n", h=IH)
            q4 = qq.rearrange("p b (h n) -> p b h n", h=HEADS)
            ki3 = kiwi[:, :, 0:64]
            wi3 = kiwi[:, :, 64:68]
            dve.wait_ge(job_read, 2)
            head_squares(k4, KV, 132)
            dve.wait_ge(job_read, 4)
            step(V.tensor_reduce(out=small[:, 192:194], in_=ki3, op=ALU.add, axis=AX))
            step(V.tensor_scalar(small[:, 192:194], small[:, 192:194], -1.0 / ID, None, ALU.mult))
            step(V.tensor_tensor(ki3, ki3, small[:, 192:194].unsqueeze(2).to_broadcast([P, NB, ID]), ALU.add))
            step(V.tensor_tensor(v3(rtmp[3][:, 0:NB * ID], NB), ki3, ki3, ALU.mult))
            step(V.tensor_reduce(out=small[:, 136:138], in_=v3(rtmp[3][:, 0:NB * ID], NB), op=ALU.add, axis=AX))
            root_and_reciprocal(132, 6, 1.0 / HD, 2)
            scaled(k4, KV, 132, rows[:, R_KG:R_KG + HD])
            dve.wait_ge(trig_ready, 2)
            rope(k4, [kdup[:, :, :, 0:64], kdup[:, :, :, 64:128]], KV, 32, 1).then_inc(roped, 1)
            dve.wait_ge(roped, 1)
            step(V.tensor_tensor(ki3, ki3, small[:, 136:138].unsqueeze(2).to_broadcast([P, NB, ID]), ALU.mult))
            step(V.tensor_tensor(ki3, ki3, rows[:, R_IG:R_IG + ID].unsqueeze(1).to_broadcast([P, NB, ID]), ALU.mult))
            step(V.tensor_tensor(ki3, ki3, rows[:, R_IB:R_IB + ID].unsqueeze(1).to_broadcast([P, NB, ID]), ALU.add))
            kd4 = kidup.rearrange("p b (r n) -> p b r n", r=2)
            rope(ki3.unsqueeze(2), [kd4[:, :, 0:1, :], kd4[:, :, 1:2, :]], 1, 16, 2)
            V.tensor_copy(kd4[:, :, 0, IROPE:], ki3[:, :, IROPE:])
            V.tensor_copy(kd4[:, :, 1, IROPE:], ki3[:, :, IROPE:]).then_inc(roped, 1)
            dve.wait_ge(roped, 2)
            rope(qi4, [qi4], IH, 16, 2).then_inc(roped, 1)
            dve.wait_ge(roped, 3)
            step(V.tensor_scalar(wi3, wi3, IDX_SCALE, None, ALU.mult))
            dve.wait_ge(job_read, 6)
            head_squares(q4, HEADS, 140)
            root_and_reciprocal(140, 16, 1.0 / HD, 3)
            scaled(q4, HEADS, 140, rows[:, R_QG:R_QG + HD])
            rope(q4, [q4], HEADS, 32, 1).then_inc(roped, 1)
            dve.wait_ge(roped, 4)
            for b in range(NB):
                nk = P * (b + 1)
                short_read(dve, (TJ_L0, TJ_L1)[b] + 2)
                step(V.tensor_scalar(score[:, b, 0:nk], relu[:, 0, 0:nk], wi3[:, b, 0:1], None, ALU.mult))
                for h in range(1, IH):
                    ins = V.scalar_tensor_tensor(out=score[:, b, 0:nk], in0=relu[:, h, 0:nk], scalar=wi3[:, b, h:h + 1],
                                                 in1=score[:, b, 0:nk], op0=ALU.mult, op1=ALU.add)
                    if h < IH - 1:
                        step(ins)
                ins.then_inc(relu_used, 1)
                dve.wait_ge(relu_used, b + 1)
                step(V.memset(score[0:CHUNK, b, nk - CHUNK:nk], NEG_MASK))
                top = small[:, 196:204]
                src = score[:, b, 0:nk]
                for r in range(N_SEL // 8):
                    step(V.max(out=top, in_=src))
                    step(V.match_replace(out=work[:, b, 0:nk], in_to_replace=top, in_values=src, imm_value=REPL))
                    src = work[:, b, 0:nk]
                step(V.tensor_scalar(pen[:, b, 0:nk], work[:, b, 0:nk], -3.395e38, -1.0e30, ALU.is_gt, ALU.mult))
            for b in range(NB):
                nk = P * (b + 1)
                per = BANK // nk
                first = TJ_S0 if b == 0 else TJ_S1
                if b == 1:
                    dve.wait_ge(t_ready, TJ_X + 4)
                for j in range(HEADS // per):
                    dve.wait_ge(t_ready, first + j + 1)
                    h0 = 4 * (j // 2) + j % 2 if b == 1 else j
                    V.scalar_tensor_tensor(out=att[b][:, h0:h0 + 2 * per - 1:2, :], in0=v3(TB[(first + j) % 2][:, :], per),
                                           scalar=SCALE, in1=pen[:, b, 0:nk].unsqueeze(1).to_broadcast([P, per, nk]),
                                           op0=ALU.mult, op1=ALU.add).then_inc(t_read[(first + j) % 2], 1)
                short_read(dve, first + HEADS // per)
                mx = small[:, 156 + 8 * b:164 + 8 * b]
                step(V.tensor_reduce(out=mx, in_=att[b], op=ALU.max, axis=AX))
                V.tensor_scalar(mx, mx, -1.0, None, ALU.mult).then_inc(att_masked, 1)
            for b in range(NB):
                nk = P * (b + 1)
                sums = small[:, 172 + 8 * b:180 + 8 * b]
                dve.wait_ge(att_exp, 8 * (b + 1))
                step(V.reciprocal(sums, sums))
                V.tensor_tensor(att[b], att[b], sums.unsqueeze(2).to_broadcast([P, HEADS, nk]), ALU.mult).then_inc(prob_ready, 1)

            def tcopy(j, dst):
                dve.wait_ge(t_ready, j + 1)
                V.tensor_copy(dst, v3(TB[j % 2][:, :], 4)).then_inc(t_read[j % 2], 1)

            tcopy(TJ_P0 + 1, PT[0][:, 0, 4:8, :])
            tcopy(TJ_P1 + 1, PT[1][:, 0, 4:8, :])
            tcopy(TJ_P1 + 3, PT[1][:, 1, 4:8, :])
            for j in range(2):
                dve.wait_ge(t_ready, TJ_POOL + j + 1)
                V.tensor_tensor(pooledT[:, 2 * j:2 * j + 2, :], v3(TB[(TJ_POOL + j) % 2][:, :], 2),
                                cols[:, P_PS + 2 * j:P_PS + 2 * j + 2].unsqueeze(2).to_broadcast([P, 2, SEQ]),
                                ALU.mult).then_inc(t_read[(TJ_POOL + j) % 2], 1)
            dve.wait_ge(job_read, 16)

            def gated(j0, b, gate):
                j = j0 + b
                for h in range(2):
                    dve.wait_ge(job_ready, 2 * j + 1 + h)
                    V.tensor_tensor(gate[:, b, 512 * h:512 * h + 512], bank[PAIR_BANKS[j % 3][h]][:, :],
                                    gate[:, b, 512 * h:512 * h + 512], ALU.mult).then_inc(job_read, 1)

            for b in range(NB):
                gated(BJ_WA, b, siga)
            for b in range(NB):
                gated(BJ_WB, b, sigp)
                dve.wait_ge(job_read, 2 * (BJ_WB + b) + 2)
                V.tensor_tensor(siga[:, b, :], siga[:, b, :], sigp[:, b, :], ALU.add).then_inc(merged_ready, 1)
            for j in (1, 3):
                tcopy(TJ_M + j, hT[:, 4:8, (j // 2) * P:(j // 2) * P + P])
            for b in range(NB):
                j = BJ_WO + b
                for h in range(2):
                    dve.wait_ge(job_ready, 2 * j + 1 + h)
                    V.tensor_tensor(x[:, b, 512 * h:512 * h + 512], bank[PAIR_BANKS[j % 3][h]][:, :],
                                    x[:, b, 512 * h:512 * h + 512], ALU.add).then_inc(job_read, 1)
                dve.wait_ge(job_read, 2 * j + 2)
                dve.sem_inc(x2_ready, 1)
                if b == 0:
                    for g in range(2):
                        gained(TJ_H2 + g, 4 * g, 0, P_G2)
            for g in range(2):
                gained(TJ_H2 + 2 + g, 4 * g, 1, P_G2)
            dve.wait_ge(xn_ready, 2 * NB)
            root_and_reciprocal(128, 2, 1.0 / D, 4)
            lgp = v3(rt_t[:, 0:80], NB)
            rex = v3(rt_t[:, 128:192], NB)
            rwork = v3(rt_t[:, 192:256 + 16], NB)
            rwork = v3(rt_t[:, 512:592], NB)
            msk = v3(rt_t[:, 640:704], NB)
            gex = v3(rt_t[:, 704:768], NB)
            step(V.memset(lgp[:, :, E:E + 8], PAD))
            dve.wait_ge(t_ready, TJ_R + 1)
            lgs = v3(TB[TJ_R % 2][:, 0:SEQ], NB)[:, :, 0:E]
            for b in range(NB):
                ins = V.scalar_tensor_tensor(out=lgp[:, b, 0:E], in0=lgs[:, b, :], scalar=small[:, 128 + b:129 + b],
                                             in1=rows[:, R_RB:R_RB + E], op0=ALU.mult, op1=ALU.add)
            ins.then_inc(t_read[TJ_R % 2], 1)
            dve.wait_ge(t_read[TJ_R % 2], TJ_R // 2 + 1)
            tops = small[:, 204:220]
            for b in range(NB):
                step(V.max(out=tops[:, 8 * b:8 * b + 8], in_=lgp[:, b, 0:E]))
                step(V.memset(tops[:, 8 * b + TOPK:8 * b + 8], PAD))
            V.tensor_scalar(small[:, 190:192], v3(tops, NB)[:, :, 0], -1.0, None, ALU.mult).then_inc(lg_ready, 1)
            for b in range(NB):
                step(V.match_replace(out=rwork[:, b, :], in_to_replace=tops[:, 8 * b:8 * b + 8], in_values=lgp[:, b, :], imm_value=REPL))
            step(V.tensor_scalar(msk, rwork[:, :, 0:E], -3.395e38, None, ALU.is_lt))
            dve.wait_ge(ex_ready, 2)
            step(V.tensor_tensor(gex, rex, msk, ALU.mult))
            step(V.tensor_reduce(out=small[:, 220:222], in_=gex, op=ALU.add, axis=AX))
            step(V.reciprocal(small[:, 220:222], small[:, 220:222]))
            V.tensor_tensor(gat, gex, small[:, 220:222].unsqueeze(2).to_broadcast([P, NB, E]), ALU.mult).then_inc(gates_ready, 1)
            notm = v3(rt_t[:, 768:832], NB)
            step(V.tensor_scalar(notm, msk, -BIG_RANK, BIG_RANK, ALU.mult, ALU.add))
            dve.wait_ge(t_ready, TJ_RANK + 1)
            ranks = v3(TB[TJ_RANK % 2][:, 0:SEQ], NB)[:, :, 0:E]
            step(V.tensor_tensor(rank, ranks, notm, ALU.add))
            step(V.tensor_reduce(out=small[:, 222:223], in_=TB[TJ_RANK % 2][:, SEQ:SEQ + E], op=ALU.max, axis=AX))
            cnt = small[:, 222:223]
            step(V.tensor_scalar(small[:, 223:224], cnt, float(T), None, ALU.is_gt))
            for r in (2, 3):
                step(V.scalar_tensor_tensor(out=small[:, 223:224], in0=cnt, scalar=float(r * T), in1=small[:, 223:224], op0=ALU.is_gt, op1=ALU.add))
            V.tensor_scalar(n_t[:, :], small[:, 223:224], float(PAIRS), float(PAIRS), ALU.mult, ALU.add).then_inc(n_ready, 1)
            dve.wait_ge(n_ready, 1)
            dve.sem_inc(t_read[TJ_RANK % 2], 1)
            iota4 = iota.unsqueeze(1).unsqueeze(1).to_broadcast([P, NB, 2, T])

            def make_sel(p):
                r = rank[:, :, bass.ds(2 * p, 2)].unsqueeze(3).to_broadcast([P, NB, 2, T])
                V.tensor_tensor(sel, iota4, r, ALU.is_equal).then_inc(sel_ready, 1)

            def take_xgT(count):
                for h in range(2):
                    dve.wait_ge(done[f"X{h}"], count)
                    g = cols[:, P_G2 + 4 * h:P_G2 + 4 * h + 4].unsqueeze(2).to_broadcast([P, 4, P])
                    V.tensor_tensor(xgT[:, 4 * h:4 * h + 4, :], v3(TB[h][:, :], 4), g, ALU.mult).then_inc(read[f"X{h}"], 1)

            make_sel(0)
            for b in range(NB):
                j = BJ_BD + b
                dve.wait_ge(job_ready, 2 * j + 2)
                for h in range(2):
                    V.tensor_tensor(x[:, b, 512 * h:512 * h + 512], bank[PAIR_BANKS[j % 3][h]][:, :],
                                    x[:, b, 512 * h:512 * h + 512], ALU.add).then_inc(job_read, 1)
            dve.wait_ge(job_read, 2 * (BJ_BD + 2))

            take_xgT(1)
            n = dve.value_load(n_t[0:1, 0:1], min_val=PAIRS, max_val=4 * PAIRS)
            with dve.Fori(0, n) as it:
                c1 = dve.snap(it + 1)
                c2 = dve.snap(it + 2)
                here = dve.snap(it % PAIRS)
                after = dve.snap((it + 1) % PAIRS)
                dve.wait_ge(sel_ready, c1)
                dve.wait_ge(read["Y3"], c1)
                g = gat[:, :, bass.ds(2 * here, 2)].unsqueeze(3).to_broadcast([P, NB, 2, T])
                V.tensor_tensor(selg, sel, g, ALU.mult).then_inc(selg_ready, 1)
                rk = rank[:, :, bass.ds(2 * here, 2)]
                V.tensor_scalar(rk, rk, float(T), None, ALU.subtract).then_inc(rank_down, 1)
                dve.wait_ge(selg_ready, c1)
                dve.wait_ge(rank_down, c1)
                dve.wait_ge(done["G1"], c1)
                make_sel(after)

                def swiglu(e):
                    name = "AB"[e]
                    cnt = dve.snap(2 * it + 1 + e)
                    if e == 1:
                        dve.wait_ge(act_ready, dve.snap(2 * it + 2))
                    for h in range(2):
                        j = f"T{name}{h}"
                        dve.wait_ge(done[j], c1)
                        bias = bgu[:, bass.ds(2 * here + e, 1), 4 * h:4 * h + 4, :].rearrange("p e c g -> p (e c) g")
                        V.tensor_tensor(gu1[:, 4 * h:4 * h + 4, :, :], v4(TB[h][:, :], 4, 2),
                                        bias.unsqueeze(3).to_broadcast([P, 4, 2, T]), ALU.add).then_inc(read[j], 1)
                    for h in range(2):
                        dve.wait_ge(read[f"T{name}{h}"], c1)
                    V.tensor_scalar(gu1[:, :, 0, :], gu1[:, :, 0, :], LIMIT, None, ALU.min).then_inc(clipped, 1)
                    V.tensor_scalar(up1, gu1[:, :, 1, :], LIMIT, -LIMIT, ALU.min, ALU.max).then_inc(up_ready, 1)
                    dve.wait_ge(clipped, cnt)
                    dve.wait_ge(up_ready, cnt)
                    V.scalar_tensor_tensor(out=up1, in0=up1, scalar=1.0, in1=gu1[:, :, 0, :],
                                           op0=ALU.add, op1=ALU.mult).then_inc(prod_ready, 1)
                    dve.wait_ge(prod_ready, cnt)
                    dve.wait_ge(sig_ready, cnt)
                    V.tensor_tensor(actT[:, :, T * e:T * e + T], up1, sg, ALU.mult).then_inc(act_ready, 1)

                swiglu(0)
                swiglu(1)
                take_xgT(c2)
                dve.wait_ge(down_done, c1)
                V.tensor_copy(dsb[:, 512:1024], bank[5][:, :]).then_inc(d_copied[1], 1)
                for j in range(4):
                    b, h = j // 2, j % 2
                    dve.wait_ge(done[f"Y{j}"], c1)
                    V.tensor_tensor(x[:, b, 512 * h:512 * h + 512], TB[h][:, :], x[:, b, 512 * h:512 * h + 512],
                                    ALU.add).then_inc(read[f"Y{j}"], 1)

        @block.tensor
        def _(pe):
            MM = nc.tensor.matmul
            tj = [0]

            def t_job(j):
                assert j == tj[0], (j, tj[0])
                tj[0] += 1
                if j >= 2:
                    pe.wait_ge(t_read[j % 2], j // 2)
                return TB[j % 2]

            def transposes(j, srcs):
                dst = t_job(j)
                for k, s in enumerate(srcs):
                    ins = nc.tensor.transpose(dst[:, k * P:k * P + P], s, ident)
                ins.then_inc(t_ready, 1)

            def unit(u):
                s = u % SLOTS
                pe.wait_ge(unit_in[s], 16 * (u // SLOTS + 1))
                return ring[s]

            def free_unit(u, ins):
                ins.then_inc(unit_used[u % SLOTS], 1)

            def free_banks(j):
                if j >= 3:
                    pe.wait_ge(job_read, 2 * (j - 2))

            def projection(j):
                free_banks(j)
                n = groups[j][1]
                for half in range(2):
                    u = 2 * j + half
                    w = v3(unit(u)[:, 0:4 * n], 4)
                    for b in range(NB):
                        for k in range(4):
                            kc = 4 * half + k
                            ins = MM(bank[PAIR_BANKS[j % 3][b]][:, 0:n], hT[:, kc, b * P:b * P + P], w[:, k, :],
                                     start=kc == 0, stop=kc == KC - 1)
                        if half == 0 and b == 1:
                            free_unit(u, ins)
                        if half == 1:
                            ins.then_inc(job_ready, 1)
                    if half == 1:
                        pe.wait_ge(job_ready, 2 * j + 2)
                        pe.sem_inc(unit_used[u % SLOTS], 1)

            def branch(b, j0, u0, nk, lhs, between=None):
                j = j0 + b
                free_banks(j)
                for k in range(nk):
                    if between is not None and k == nk // 2:
                        between()
                    u = u0 + k // 2
                    w = v3(unit(u)[:, :], 2)
                    for h in range(2):
                        ins = MM(bank[PAIR_BANKS[j % 3][h]][:, :], lhs[:, k, b * P:b * P + P], w[:, k % 2, 512 * h:512 * h + 512],
                                 start=k == 0, stop=k == nk - 1)
                        if k == nk - 1:
                            ins.then_inc(job_ready, 1)
                    if b == NB - 1 and k % 2 == 1 and k < nk - 1:
                        free_unit(u, ins)
                if b == NB - 1:
                    pe.wait_ge(job_ready, 2 * (j0 + NB))
                    pe.sem_inc(unit_used[(u0 + nk // 2 - 1) % SLOTS], 1)

            pe.wait_ge(ident_in, 16)
            for b in range(NB):
                pe.wait_ge(x_in[b], 16)
                for g in range(2):
                    transposes(TJ_X + 2 * b + g, [x[:, b, (4 * g + k) * P:(4 * g + k + 1) * P] for k in range(4)])
            short_read(pe, TJ_X + 4)
            for j in range(4):
                projection(j)
            pe.wait_ge(roped, 1)
            transposes(TJ_K, [kdup[:, b, kv, :] for b in range(NB) for kv in range(KV)])
            pe.wait_ge(roped, 3)
            transposes(TJ_QI, [kvqi[:, b, 256 + P * g:256 + P * g + P] for b in range(NB) for g in range(2)])
            transposes(TJ_KI, [kidup[:, b, :] for b in range(NB)])
            short_read(pe, TJ_KI + 1)
            for b in range(NB):
                nk = P * (b + 1)
                for par in range(2):
                    dst = t_job((TJ_L0, TJ_L1)[b] + par)
                    for i in range(2):
                        h = 2 * i + par
                        r = 64 * (h % 2)
                        ins = MM(dst[:, i * nk:i * nk + nk], qiT[r:r + 64, h // 2, b * P:b * P + P], kiT_t[r:r + 64, 0:nk],
                                 start=True, stop=True)
                    ins.then_inc(t_ready, 1)
            projection(4)
            pe.wait_ge(roped, 4)
            for b in range(NB):
                transposes(TJ_Q + b, [qq[:, b, P * g:P * g + P] for g in range(4)])
            projection(5)
            short_read(pe, TJ_Q + 2)
            for b in range(NB):
                nk = P * (b + 1)
                per = BANK // nk
                for g in range(HEADS // per):
                    dst = t_job((TJ_S0 if b == 0 else TJ_S1) + g)
                    h0 = 4 * (g // 2) + g % 2 if b == 1 else g
                    for i in range(per):
                        h = h0 + 2 * i
                        r = 64 * (h % 2)
                        ins = MM(dst[:, i * nk:i * nk + nk], qT[r:r + 64, h // 2, b * P:b * P + P], kT[r:r + 64, h // 4, 0:nk],
                                 start=True, stop=True)
                    ins.then_inc(t_ready, 1)
            projection(6)
            for b in range(NB):
                pe.wait_ge(prob_ready, b + 1)
                for kb in range(b + 1):
                    for g in range(2):
                        transposes((TJ_P0 if b == 0 else TJ_P1) + 2 * kb + g,
                                   [att[b][:, 4 * g + i, kb * P:kb * P + P] for i in range(4)])
            projection(7)
            pe.wait_ge(late_in, 48)
            pe.wait_ge(job_read, 8)
            for j in range(2):
                dst = t_job(TJ_MIX + j)
                for i in range(2):
                    g = 2 * j + i
                    MM(dst[:, i * SEQ:i * SEQ + P], pool[:, 0, g * P:g * P + P], bands[:, g, 0, :], start=True, stop=True)
                    MM(dst[:, i * SEQ + P:(i + 1) * SEQ], pool[:, 0, g * P:g * P + P], bands[:, g, 1, :], start=True, stop=False)
                    ins = MM(dst[:, i * SEQ + P:(i + 1) * SEQ], pool[:, 1, g * P:g * P + P], bands[:, g, 2, :], start=False, stop=True)
                ins.then_inc(t_ready, 1)
            for b in range(NB):
                dst = t_job(TJ_O + b)
                for kv in range(KV):
                    for par in range(2):
                        for kb in range(b + 1):
                            h0 = 4 * kv + par
                            ins = MM(dst[64 * par:64 * par + 64, kv * 2 * P:(kv + 1) * 2 * P],
                                     kvqi[:, kb, P + 64 * kv:P + 64 * kv + 64], PT[b][:, kb, h0:h0 + 3:2, :],
                                     start=kb == 0, stop=kb == b)
                ins.then_inc(t_ready, 1)
            for j in range(2):
                dst = t_job(TJ_POOL + j)
                for i in range(2):
                    g = 2 * j + i
                    ins = MM(dst[:, i * SEQ:(i + 1) * SEQ], mixw[:, g, :], mixedT[:, g, :], start=True, stop=True)
                ins.then_inc(t_ready, 1)
            for b in range(NB):
                branch(b, BJ_WA, 16, 4, attnT)
            short_read(pe, TJ_POOL + 2)
            for b in range(NB):
                branch(b, BJ_WB, 18, 4, pooledT)

            def turn_merged(b):
                pe.wait_ge(merged_ready, b + 1)
                for g in range(2):
                    transposes(TJ_M + 2 * b + g, [siga[:, b, (4 * g + k) * P:(4 * g + k + 1) * P] for k in range(4)])

            def turn_x2(b):
                pe.wait_ge(x2_ready, b + 1)
                for g in range(2):
                    transposes(TJ_H2 + 2 * b + g, [x[:, b, (4 * g + k) * P:(4 * g + k + 1) * P] for k in range(4)])

            turn_merged(0)
            short_read(pe, TJ_M + 2)
            branch(0, BJ_WO, 20, 8, hT, lambda: turn_merged(1))
            short_read(pe, TJ_M + 4)
            branch(1, BJ_WO, 20, 8, hT, lambda: turn_x2(0))
            turn_x2(1)
            pe.wait_ge(rw_in, 16)
            dst = t_job(TJ_R)
            short_read(pe, TJ_H2 + 4)
            for b in range(NB):
                for k in range(KC):
                    ins = MM(dst[:, b * P:b * P + E], hT[:, k, b * P:b * P + P], rw[:, k, :], start=k == 0, stop=k == KC - 1)
            ins.then_inc(t_ready, 1)
            pe.wait_ge(gates_ready, 1)
            dst = t_job(TJ_RANK)
            msk = v3(rt_t[:, 640:704], NB)
            MM(dst[:, 0:E], tri, msk[:, 0, :], start=True, stop=True)
            MM(dst[:, P:P + E], ones, msk[:, 0, :], start=True, stop=False)
            MM(dst[:, P:P + E], tri, msk[:, 1, :], start=False, stop=True)
            MM(dst[:, SEQ:SEQ + E], ones, msk[:, 0, :], start=True, stop=False)
            MM(dst[:, SEQ:SEQ + E], ones, msk[:, 1, :], start=False, stop=True).then_inc(t_ready, 1)
            dst = t_job(TJ_G)
            for b in range(NB):
                ins = MM(dst[0:E, b * P:b * P + P], gat[:, b, :], ident, start=True, stop=True)
            ins.then_inc(t_ready, 1)
            pe.wait_ge(bd_in, 16)
            short_read(pe, TJ_G + 1)

            pe.wait_ge(xn_ready, 3 * NB)

            def gather(count):
                pe.wait_ge(sel_ready, count)
                for h in range(2):
                    for b in range(NB):
                        ins = MM(TB[h][:, :], selb[:, b * P:b * P + P], xn[:, b, 512 * h:512 * h + 512], start=b == 0, stop=b == NB - 1)
                    ins.then_inc(done[f"G{h}"], 1)

            def turn(name, src, h):
                for k in range(4):
                    c = 4 * h + k
                    ins = nc.tensor.transpose(TB[h][:, k * P:k * P + P], src[:, c * P:c * P + P], ident)
                ins.then_inc(done[f"{name}{h}"], 1)

            gather(1)
            for b in range(NB):
                j = BJ_BD + b
                free_banks(j)
                for h in range(2):
                    MM(bank[PAIR_BANKS[j % 3][h]][:, :], rt_t[0:E, 256 + b * P:256 + b * P + P], bd_sb[:, 512 * h:512 * h + 512],
                       start=True, stop=True).then_inc(job_ready, 1)
            for h in range(2):
                pe.wait_ge(read["G0"], 1)
                pe.wait_ge(read["G1"], 1)
                turn("X", xg, h)
            pe.wait_ge(job_read, 2 * (BJ_BD + 2))
            n = pe.value_load(n_t[0:1, 0:1], min_val=PAIRS, max_val=4 * PAIRS)
            with pe.Fori(0, n) as it:
                c1 = pe.snap(it + 1)
                c2 = pe.snap(it + 2)
                a3 = pe.snap(2 * it + 3)
                in1 = pe.snap(32 * it + 48)
                in2 = pe.snap(32 * it + 64)

                def gate_up(e, k):
                    u = 8 * e + k
                    s = u % SLOTS
                    pe.wait_ge(unit_in[s], in1 if u < SLOTS else in2)
                    for h in range(2):
                        for g in range(2):
                            ins = MM(bank[2 * e + h][T * g:T * g + T, :], xgT[:, k, T * e:T * e + T],
                                     ring[s][:, D * g + 512 * h:D * g + 512 * h + 512], start=k == 0, stop=k == KC - 1)
                    ins.then_inc(unit_used[s], 1)

                pe.wait_ge(read["X0"], c1)
                pe.wait_ge(read["X1"], c1)
                pe.wait_ge(gu_copied[0], c1)
                for k in range(KC):
                    gate_up(0, k)
                pe.wait_ge(unit_used[7], pe.snap(2 * it + 3))
                pe.sem_inc(gu_done[0], 1)
                pe.wait_ge(gu_copied[1], c1)
                for k in range(2):
                    gate_up(1, k)
                pe.wait_ge(gu_copied[0], c2)
                pe.wait_ge(read["Y2"], c1)
                turn("TA", gu_sb, 0)
                pe.wait_ge(read["Y3"], c1)
                turn("TA", gu_sb, 1)
                pe.wait_ge(selg_ready, c1)
                for b in range(NB):
                    pe.wait_ge(read[f"TA{b}"], c1)
                    nc.tensor.transpose(TB[b][:, 0:P], selgb[:, b * P:b * P + P], ident).then_inc(done[f"S{b}"], 1)
                for k in range(2, KC):
                    gate_up(1, k)
                pe.wait_ge(unit_used[3], pe.snap(2 * it + 4))
                pe.sem_inc(gu_done[1], 1)
                pe.wait_ge(read["S0"], c1)
                pe.wait_ge(read["S1"], c1)
                gather(c2)
                pe.wait_ge(gu_copied[1], c2)
                for h in range(2):
                    pe.wait_ge(read[f"G{h}"], c2)
                    turn("TB", gu_sb, h)
                for h in range(2):
                    pe.wait_ge(read[f"TB{h}"], c1)
                    turn("X", xg, h)
                pe.wait_ge(act_ready, a3)
                pe.wait_ge(d_copied[0], c1)
                pe.wait_ge(d_copied[1], c1)
                for k2 in range(KC // 2):
                    ws = []
                    for e in range(2):
                        u = 16 + 2 * k2 + e
                        pe.wait_ge(unit_in[u % SLOTS], in2)
                        ws.append(v3(ring[u % SLOTS][:, :], 2))
                    for k in range(2):
                        c = 2 * k2 + k
                        for h in range(2):
                            for e in range(2):
                                ins = MM(bank[4 + h][T * e:T * e + T, :], actT[:, c, T * e:T * e + T],
                                         ws[e][:, k, 512 * h:512 * h + 512], start=c == 0, stop=c == KC - 1)
                                if k == 1 and h == 1:
                                    ins.then_inc(unit_used[(16 + 2 * k2 + e) % SLOTS], 1)
                pe.wait_ge(unit_used[SLOTS - 1], pe.snap(2 * it + 4))
                pe.sem_inc(down_done, 1)
                pe.wait_ge(d_copied[0], c2)
                pe.wait_ge(d_copied[1], c2)
                for j in range(4):
                    b, h = j // 2, j % 2
                    if b == 0:
                        pe.wait_ge(read[f"X{h}"], c2)
                    else:
                        pe.wait_ge(read[f"Y{h}"], c2)
                    MM(TB[h][:, :], selgT[:, b * P:b * P + P], dsb[:, 512 * h:512 * h + 512],
                       start=True, stop=True).then_inc(done[f"Y{j}"], 1)


def constant_tables():
    import numpy as np
    t = np.zeros((P, K_W), np.float32)
    t[:, K_IDENT:K_IDENT + P] = np.eye(P)
    t[:, K_TRI:K_TRI + P] = np.triu(np.ones((P, P)), 1)
    t[:, K_ONES:K_ONES + P] = 1.0
    t[:, K_IOTA:K_IOTA + T] = np.arange(T)
    t[:, K_INVF:K_INVF + 32] = np.power(np.float32(10000.0), -(np.arange(0, HD, 2, dtype=np.float32) / np.float32(HD)))
    bands = np.zeros((GROUPS, SEQ, SEQ), np.float32)
    for g, w in enumerate(WINDOWS):
        for s in range(SEQ):
            lo = max(s + 1 - w, 0)
            bands[g, lo:s + 1, s] = 1.0 / (s + 1 - lo)
            bands[g, s, s] -= 1.0
    b = np.stack([bands[:, :P, :P], bands[:, :P, P:], bands[:, P:, P:]], axis=1)
    return t, np.ascontiguousarray(b.transpose(2, 0, 1, 3).reshape(P, GROUPS * 3 * P))


def kernel(**inputs):
    import numpy as np
    import concourse.bacc as bacc
    from concourse import mybir as mb
    from concourse.bass_utils import run_bass_kernel_spmd

    a = {k: np.ascontiguousarray(v) for k, v in inputs.items()}
    consts, bands = constant_tables()
    rows = np.concatenate([a[k].reshape(-1) for k in ("q_norm_g", "k_norm_g", "idx_k_norm_g", "idx_k_norm_b", "router_b")])
    cols = np.concatenate([a["norm1_g"].reshape(KC, P).T, a["pool_scale"].reshape(GROUPS, P).T,
                           a["norm2_g"].reshape(KC, P).T], axis=1)
    bgu = a["b_gate_up"].reshape(E, 2, KC, P).transpose(3, 0, 2, 1).reshape(P, E * KC * 2)
    arrays = {
        "x": a["x"].reshape(SEQ, D), "positions": a["positions"].reshape(NB, P).T, "w_in": a["w_in"].reshape(D, IN_W),
        "w_branch_attn": a["w_branch_attn"].reshape(512, D), "w_branch_pool": a["w_branch_pool"].reshape(512, D),
        "w_out": a["w_out"].reshape(D, D), "pool_mix_w": a["pool_mix_w"].reshape(GROUPS, P, P),
        "router_w": a["router_w"].reshape(D, E), "w_gate_up": a["w_gate_up"].reshape(E * D, 2 * D),
        "w_down": a["w_down"].reshape(E * D, D), "b_down": a["b_down"].reshape(E, D),
        "consts": consts, "bands": bands, "rows": rows.reshape(1, R_W), "cols": cols, "bgu": bgu,
    }
    arrays = {f"{k}_dram": np.ascontiguousarray(v) for k, v in arrays.items()}
    nc = bacc.Bacc("TRN2", target_bir_lowering=False, num_devices=1)
    args = [nc.dram_tensor(k, v.shape, mb.dt.from_np(v.dtype), kind="ExternalInput").ap() for k, v in arrays.items()]
    out = nc.dram_tensor("out_dram", (SEQ, D), mb.dt.float32, kind="ExternalOutput").ap()
    block_kernel(nc, *args, out)
    r = run_bass_kernel_spmd(nc, [arrays], core_ids=[0])
    return r.results[0]["out_dram"].reshape(1, SEQ, D)
```

```python
import concourse.bass as bass
from concourse import mybir
from contextlib import ExitStack

P = 128
SEQ = 256
D = 1024
NB = SEQ // P
KC = D // P
HEADS, KV, HD = 8, 2, 64
IH, ID, IROPE = 4, 64, 32
CHUNK = 64
N_SEL = 64
GROUPS, PW = 4, 512
WINDOWS = (2, 4, 8, 16)
E, TOPK = 32, 4
T = 64
PAIRS = E // 2
BANK = 512
C_Q, C_K, C_QI, C_KI, C_POOL, C_GA, C_GP = 0, 512, 768, 1024, 1092, 1604, 2628
IN_W = 3652
EPS = 1e-6
SCALE = HD ** -0.5
IDX_SCALE = (IH ** -0.5) * (ID ** -0.5)
ALPHA, LIMIT = 1.702, 7.0

K_IDENT, K_TRI, K_ONES, K_IOTA, K_INVF = 0, 128, 256, 384, 448
K_W = 480
R_QG, R_KG, R_IG, R_IB, R_RB = 0, 64, 128, 192, 256
R_W = 288
P_G1, P_PS, P_G2 = 0, 8, 12
P_W = 20

RING = 12
EXTRA = 4
SLOTS = RING + EXTRA
PRE_UNITS = 24
PAIR_UNITS = 24
UW = 2048

NEG_MASK = -3.0e38
REPL = -3.4e38
PAD = -3.39e38
BIG_RANK = 1.0e6
TWO_PI = 6.283185307179586
MAGIC = 12582912.0


def two_pi_parts():
    import numpy as np
    c1 = 6.28125
    c2 = float(np.float32(np.floor((TWO_PI - c1) * 2.0 ** 21) / 2.0 ** 21))
    c3 = float(np.float32(TWO_PI - c1 - c2))
    return c1, c2, c3


def block_kernel(nc, x_d, pos_d, w_in, w_a, w_b, w_out, mix_d, router_d, w_gu, w_dn, b_dn,
                 consts_d, bands_d, rows_d, cols_d, bgu_d, out_d):
    f32, i32 = mybir.dt.float32, mybir.dt.int32
    ALU = mybir.AluOpType
    ACT = mybir.ActivationFunctionType
    AX = mybir.AxisListType.X
    ctx = ExitStack()
    with ctx:
        def sb(name, width, dt=f32, parts=P):
            return ctx.enter_context(nc.sbuf_tensor(name, [parts, width], dt))

        def sem(name):
            return ctx.enter_context(nc.semaphore(name))

        def v3(ap, a):
            return ap.rearrange("p (a n) -> p a n", a=a)

        def v4(ap, a, b):
            return ap.rearrange("p (a b n) -> p a b n", a=a, b=b)

        ring = [sb(f"ring{s}", UW) for s in range(RING)]
        consts = sb("consts", K_W)
        rows = sb("rows", R_W)
        cols = sb("cols", P_W)
        bgu_t = sb("bgu", E * KC * 2)
        small = sb("small", 256)
        x_t = sb("x", NB * D)
        xn_t = sb("xn", NB * D)
        hT_t = sb("hT", KC * SEQ)
        siga_t = sb("siga", NB * D)
        sigp_t = sb("sigp", NB * D)
        kvqi_t = sb("kvqi", NB * 512)
        kiwi_t = sb("kiwi", NB * 68)
        q_t = sb("q", NB * 512)
        pool_t = sb("pool", NB * 512)
        kdup_t = sb("kdup", NB * KV * P)
        kqT_t = sb("kqT", (KV + 2) * SEQ)
        kidup_t = sb("kidup", NB * P)
        kiT_t = sb("kiT", SEQ)
        qo_t = sb("qo", 8 * SEQ)
        qT_t, attnT_t = qo_t[:, 0:4 * SEQ], qo_t[:, 4 * SEQ:8 * SEQ]
        rt_t = sb("rt", 2 * NB * SEQ)
        big = sb("big", 6144)
        mixw_t = sb("mixw", GROUPS * P)
        posi = sb("posi", NB, i32)
        n_t = sb("n_iter", 1, i32)
        selb, selgb, selgT = (kqT_t[:, 256 * j:256 * j + 256] for j in range(3))
        rank_t = sb("rank", NB * E)
        gat_t = sb("gates", NB * E)

        ring += [siga_t, sigp_t, qo_t, hT_t]
        ident = consts[:, K_IDENT:K_IDENT + P]
        tri = consts[:, K_TRI:K_TRI + P]
        ones = consts[:, K_ONES:K_ONES + P]
        iota = consts[:, K_IOTA:K_IOTA + T]
        invf = consts[:, K_INVF:K_INVF + 32]
        x = v3(x_t[:, :], NB)
        xn = v3(xn_t[:, :], NB)
        hT = v3(hT_t[:, :], KC)
        siga, sigp = v3(siga_t[:, :], NB), v3(sigp_t[:, :], NB)
        kvqi, kiwi = v3(kvqi_t[:, :], NB), v3(kiwi_t[:, :], NB)
        qq, pool = v3(q_t[:, :], NB), v3(pool_t[:, :], NB)
        kdup = kdup_t[:, :].rearrange("p (b k c) -> p b k c", b=NB, k=KV)
        kT, qiT, qT = v3(kqT_t[:, 0:512], KV), v3(kqT_t[:, 512:1024], 2), v3(qT_t, 4)
        kidup = v3(kidup_t[:, :], NB)
        score, pen = v3(rt_t[:, 0:512], NB), v3(rt_t[:, 512:1024], NB)
        attnT = v3(attnT_t, 4)
        bands_t = big[:, 4096:5632]
        bands = v4(bands_t, GROUPS, 3)
        mixw = v3(mixw_t[:, :], GROUPS)
        relu = v3(big[:, 0:1024], 4)
        att = [v3(big[:, 0:1024], HEADS), v3(xn_t[:, :], HEADS)]
        PT = [big[:, 1024:2048].rearrange("p (k h q) -> p k h q", k=1, h=HEADS),
              big[:, 2048:4096].rearrange("p (k h q) -> p k h q", k=2, h=HEADS)]
        work = v3(big[:, 5632:6144], NB)
        mixedT, pooledT = v3(big[:, 0:1024], GROUPS), v3(big[:, 1024:2048], GROUPS)
        rtmp = [big[:, 1024 + 512 * j:1536 + 512 * j] for j in range(4)]
        angs = [big[:, 3072 + 64 * j:3136 + 64 * j] for j in range(6)]
        cos_t, sin_t = small[:, 0:64], small[:, 64:128]
        xg = big[:, 0:1024]
        xgT = v3(big[:, 1024:2048], KC)
        gu_sb = big[:, 2048:3072]
        gu1 = big[:, 3072:4096].rearrange("p (c g s) -> p c g s", c=KC, g=2)
        actT = v3(big[:, 4096:5120], KC)
        dsb = big[:, 5120:6144]
        sg = v3(kvqi_t[:, 0:512], KC)
        up1 = v3(kvqi_t[:, 512:1024], KC)
        sel = selb[:, :].rearrange("p (b e s) -> p b e s", b=NB, e=2)
        selg = selgb[:, :].rearrange("p (b e s) -> p b e s", b=NB, e=2)
        rank, gat = v3(rank_t[:, :], NB), v3(gat_t[:, :], NB)
        bgu = bgu_t[:, :].rearrange("p (e c g) -> p e c g", e=E, c=KC)
        bd_sb = q_t[0:E, :]
        rw = v3(pool_t[:, 0:KC * E], KC)

        bank = [ctx.enter_context(nc.psum_tensor(f"bank{j}", [P, BANK], f32)) for j in range(8)]
        PAIR_BANKS = [(0, 1), (2, 3), (4, 5)]
        TB = [bank[6], bank[7]]

        unit_in = [sem(f"unit_in{s}") for s in range(SLOTS)]
        unit_used = [sem(f"unit_used{s}") for s in range(SLOTS)]
        x_in = [sem("x_in0"), sem("x_in1")]
        ident_in, cols_in, small_in, late_in = sem("ident_in"), sem("cols_in"), sem("small_in"), sem("late_in")
        rw_in, bd_in = sem("rw_in"), sem("bd_in")
        dve_step = sem("dve_step")
        xn_ready = sem("xn_ready")
        t_ready = sem("t_ready")
        t_read = [sem("t_read0"), sem("t_read1")]
        job_ready, job_read = sem("job_ready"), sem("job_read")
        ms_ready, root_ready = sem("ms_ready"), sem("root_ready")
        trig_arg, trig_ready = sem("trig_arg"), sem("trig_ready")
        roped = sem("roped")
        relu_ready, relu_used = sem("relu_ready"), sem("relu_used")
        mixedT_ready = sem("mixedT_ready")
        att_masked, att_exp, prob_ready = sem("att_masked"), sem("att_exp"), sem("prob_ready")
        merged_ready, x2_ready = sem("merged_ready"), sem("x2_ready")
        lg_ready, ex_ready, gates_ready = sem("lg_ready"), sem("ex_ready"), sem("gates_ready")
        n_ready = sem("n_ready")
        chosen_ready = sem("chosen_ready")
        gatesT_ready, gatesT_read = sem("gatesT_ready"), sem("gatesT_read")
        bd_ready = sem("bd_ready")
        out_done = sem("out_done")
        sel_ready, selg_ready, rank_down = sem("sel_ready"), sem("selg_ready"), sem("rank_down")
        gu_done = [sem("guA_done"), sem("guB_done")]
        gu_copied = [[sem(f"gu{e}{h}_copied") for h in range(2)] for e in "AB"]
        clipped = sem("clipped")
        sig_ready, act_ready = sem("sig_ready"), sem("act_ready")
        up_ready, prod_ready = sem("up_ready"), sem("prod_ready")
        down_done = sem("down_done")
        d_copied = [sem("d_copied0"), sem("d_copied1")]
        JOBS = ["TA0", "TA1", "S0", "S1", "G0", "G1", "TB0", "TB1", "X0", "X1", "Y0", "Y1", "Y2", "Y3"]
        done = {j: sem(f"{j}_done") for j in JOBS}
        read = {j: sem(f"{j}_read") for j in JOBS}

        groups = [(C_K, 512), (C_KI, 68), (C_Q, 512), (C_POOL, 512),
                  (C_GA, 512), (C_GA + 512, 512), (C_GP, 512), (C_GP + 512, 512)]

        def pre_unit_src(u):
            if u < 16:
                c0, n = groups[u // 2]
                k0 = 4 * (u % 2)
                return w_in[k0 * P:(k0 + 4) * P, c0:c0 + n].rearrange("(k p) n -> p k n", p=P), n * 4
            w, r0 = [(w_a, 16), (w_b, 18), (w_out, 20)][0 if u < 18 else 1 if u < 20 else 2]
            r = (u - r0) * 2 * P
            return w[r:r + 2 * P, :].rearrange("(k p) n -> p k n", p=P), 2 * D

        def pair_unit_src(p, u):
            if u < 16:
                row = (2 * p + u // 8) * D + (u % 8) * P
                return w_gu[bass.ds(row, P), :]
            j = u - 16
            row = (2 * p + j % 2) * D + (j // 2) * 2 * P
            return w_dn[bass.ds(row, 2 * P), :].rearrange("(k p) n -> p k n", p=P)

        (TJ_X, TJ_K, TJ_QI, TJ_KI, TJ_L0, TJ_L1, TJ_Q, TJ_MIX, TJ_POOL, TJ_S0, TJ_S1,
         TJ_P0, TJ_P1, TJ_O, TJ_M, TJ_H2, TJ_R, TJ_RANK) = (
            0, 4, 5, 6, 7, 9, 11, 25, 29, 13, 15, 19, 21, 27, 31, (35, 37), (39, 40), 41)
        BJ_WA, BJ_WB, BJ_WO = 8, 10, 12

        def short_read(eng, n):
            eng.wait_ge(t_read[0], (n + 1) // 2)
            eng.wait_ge(t_read[1], n // 2)

        PRE_TURNS = PRE_UNITS // RING

        block = ctx.enter_context(nc.Block())

        @block.sync
        def _(sp):
            sp.dma_start(x[:, 0, :], x_d[0:P, :]).then_inc(x_in[0], 16)
            sp.dma_start(ident, consts_d[:, 0:P]).then_inc(ident_in, 16)
            sp.dma_start(cols[:, :], cols_d).then_inc(cols_in, 16)
            sp.dma_start(x[:, 1, :], x_d[P:2 * P, :]).then_inc(x_in[1], 16)

            for s in range(RING, SLOTS):
                sp.sem_inc(unit_in[s], 16 * PRE_TURNS)

            def pre_unit(u):
                s = u % RING
                if u >= RING:
                    sp.wait_ge(unit_used[s], u // RING)
                src, w = pre_unit_src(u)
                k = 4 if u < 16 else 2
                sp.dma_start(v3(ring[s][:, 0:w], k), src).then_inc(unit_in[s], 16)

            def pair_unit(p, v):
                s, u = v % SLOTS, v % PAIR_UNITS
                dst = ring[s][:, :] if u < 16 else v3(ring[s][:, :], 2)
                src = pair_unit_src(p if v < PAIR_UNITS else p + 1, u)
                sp.dma_start(dst, src).then_inc(unit_in[s], 16)

            for u in range(PRE_UNITS):
                pre_unit(u)
            for s in range(SLOTS):
                if s < RING:
                    sp.wait_ge(unit_used[s], PRE_TURNS)
                elif s == RING:
                    sp.wait_ge(t_ready, TJ_M + 4)
                elif s == RING + 2:
                    sp.wait_ge(job_ready, 2 * (BJ_WA + NB))
                elif s == RING + 3:
                    sp.wait_ge(t_ready, TJ_R[1] + 1)
                pair_unit(0, s)
            sp.wait_ge(n_ready, 1)
            n = sp.value_load(n_t[0:1, 0:1], min_val=PAIRS, max_val=4 * PAIRS)
            n2 = sp.snap(n // 2)

            def next_turn(p, turns, t):
                used = sp.snap(turns + (t + PRE_TURNS))
                for s in range(SLOTS):
                    sp.wait_ge(unit_used[s], used)
                    pair_unit(p, (SLOTS * t + s) % (2 * PAIR_UNITS))

            with sp.Fori(0, n2 - 1) as it:
                here = sp.snap((2 * it) % PAIRS)
                after = sp.snap((2 * it + 2) % PAIRS)
                next_turn(here, 3 * it, 1)
                next_turn(here, 3 * it, 2)
                next_turn(after, 3 * it, 3)
            next_turn(PAIRS - 2, 3 * n2, -2)
            next_turn(PAIRS - 2, 3 * n2, -1)
            credit = sp.snap(n + 1)
            for j in range(4):
                b, h = j // 2, j % 2
                sp.wait_ge(read[f"Y{j}"], credit)
                sp.dma_start(out_d[b * P:(b + 1) * P, 512 * h:512 * h + 512], x[:, b, 512 * h:512 * h + 512]).then_inc(out_done, 16)
            sp.wait_ge(out_done, 64)

        @block.gpsimd
        def _(pool_e):
            pool_e.dma_start(consts[:, P:K_W], consts_d[:, P:K_W]).then_inc(small_in, 16)
            pool_e.dma_start(rows[:, :], rows_d.to_broadcast([P, R_W])).then_inc(small_in, 16)
            pool_e.dma_start(posi[:, :], pos_d).then_inc(small_in, 16)
            pool_e.dma_start(bands_t, bands_d).then_inc(late_in, 16)
            pool_e.dma_start(mixw, mix_d.rearrange("g c d -> c g d")).then_inc(late_in, 16)
            pool_e.dma_start(bgu_t[:, :], bgu_d).then_inc(late_in, 16)
            pool_e.wait_ge(t_ready, TJ_Q + 2)
            pool_e.dma_start(q_t[0:E, :], b_dn).then_inc(bd_in, 16)
            pool_e.wait_ge(t_ready, TJ_MIX + 2)
            pool_e.dma_start(rw, router_d.rearrange("(k p) e -> p k e", p=P)).then_inc(rw_in, 16)

        @block.scalar
        def _(act):
            def root(col, n, which):
                act.wait_ge(ms_ready, which)
                nc.scalar.activation(small[:, col:col + n], small[:, col:col + n], ACT.Sqrt).then_inc(root_ready, 1)

            for j in JOBS:
                if j.startswith("Y"):
                    act.sem_inc(read[j], 1)
            for s in (*gu_copied[0], act_ready):
                act.sem_inc(s, 1)
            for b in range(NB):
                act.wait_ge(x_in[b], 16)
                nc.scalar.activation(xn[:, b, :], x[:, b, :], ACT.Square, accum_out=small[:, 128 + b:129 + b]).then_inc(xn_ready, 1)
            root(128, 2, 1)
            act.wait_ge(trig_arg, 2)
            nc.scalar.activation(sin_t, angs[1], ACT.Sin).then_inc(trig_ready, 1)
            nc.scalar.activation(cos_t, angs[3], ACT.Sin).then_inc(trig_ready, 1)

            act.wait_ge(root_ready, 2)

            def job(j, dst):
                for b in range(NB):
                    act.wait_ge(job_ready, 2 * j + b + 1)
                    n = groups[j][1]
                    src = bank[PAIR_BANKS[j % 3][b]][:, 0:n]
                    nc.scalar.activation(dst[:, b, :], src, ACT.Copy, scale=small[:, 128 + b:129 + b]).then_inc(job_read, 1)

            def gate_job(j, dst, half):
                for b in range(NB):
                    act.wait_ge(job_ready, 2 * j + b + 1)
                    src = bank[PAIR_BANKS[j % 3][b]][:, :]
                    nc.scalar.activation(dst[:, b, half * 512:half * 512 + 512], src, ACT.Sigmoid,
                                         scale=small[:, 128 + b:129 + b]).then_inc(job_read, 1)

            def tcopy(j, dst, n=BANK, func=ACT.Copy):
                act.wait_ge(t_ready, j + 1)
                src = TB[j % 2][:, 0:n]
                if len(dst.shape) == 3:
                    src = v3(src, dst.shape[1])
                if len(dst.shape) == 4:
                    src = v4(src, dst.shape[1], dst.shape[2])
                nc.scalar.activation(dst, src, func).then_inc(t_read[j % 2], 1)

            job(0, kvqi)
            job(1, kiwi)
            root(132, 6, 2)
            job(2, qq)
            root(140, 16, 3)
            job(3, pool)
            tcopy(TJ_K, kT.rearrange("p k (b t) -> p b k t", b=NB))
            tcopy(TJ_QI, qiT.rearrange("p k (b t) -> p b k t", b=NB))
            tcopy(TJ_KI, kiT_t[:, :], SEQ)
            for par in range(2):
                tcopy(TJ_L0 + par, relu[:, par::2, 0:P], 2 * P, ACT.Relu)
            act.wait_ge(relu_used, 1)
            for par in range(2):
                tcopy(TJ_L1 + par, relu[:, par::2, :], BANK, ACT.Relu)
            gate_job(4, siga, 0)
            for b in range(NB):
                tcopy(TJ_Q + b, qT[:, :, b * P:b * P + P])
            gate_job(5, siga, 1)
            for b in range(NB):
                act.wait_ge(att_masked, b + 1)
                for h in range(HEADS):
                    nc.scalar.activation(att[b][:, h, :], att[b][:, h, :], ACT.Exp,
                                         bias=small[:, 156 + 8 * b + h:157 + 8 * b + h],
                                         accum_out=small[:, 172 + 8 * b + h:173 + 8 * b + h]).then_inc(att_exp, 1)
            gate_job(6, sigp, 0)
            tcopy(TJ_P0, PT[0][:, 0, 0:4, :])
            tcopy(TJ_P1, PT[1][:, 0, 0:4, :])
            tcopy(TJ_P1 + 2, PT[1][:, 1, 0:4, :])
            gate_job(7, sigp, 1)
            for j in range(2):
                tcopy(TJ_MIX + j, mixedT[:, 2 * j:2 * j + 2, :])
            for b in range(NB):
                tcopy(TJ_O + b, attnT[:, :, b * P:b * P + P])
            for j in (0, 2):
                tcopy(TJ_M + j, hT[:, 0:4, (j // 2) * P:(j // 2) * P + P])
            for b in range(NB):
                act.wait_ge(x2_ready, b + 1)
                nc.scalar.activation(xn[:, b, :], x[:, b, :], ACT.Square, accum_out=small[:, 128 + b:129 + b]).then_inc(xn_ready, 1)
            root(128, 2, 4)
            act.wait_ge(lg_ready, 1)
            for b in range(NB):
                nc.scalar.activation(rt_t[:, 128 + 32 * b:160 + 32 * b], rt_t[:, 40 * b:40 * b + E], ACT.Exp,
                                     bias=small[:, 190 + b:191 + b]).then_inc(ex_ready, 1)
            act.wait_ge(root_ready, 8)
            act.wait_ge(xn_ready, 2 * NB)
            for b in range(NB):
                nc.scalar.activation(xn[:, b, :], x[:, b, :], ACT.Copy, scale=small[:, 128 + b:129 + b]).then_inc(xn_ready, 1)
            act.wait_ge(gatesT_ready, NB)
            nc.scalar.activation(rt_t[0:E, 256:256 + SEQ], bank[0][0:E, 0:SEQ], ACT.Copy).then_inc(gatesT_read, 1)

            def take(j, dst, src, count):
                act.wait_ge(done[j], count)
                nc.scalar.activation(dst, src, ACT.Copy).then_inc(read[j], 1)

            def take_gather(count):
                for h in range(2):
                    take(f"G{h}", xg[:, h * 512:h * 512 + 512], TB[h][:, :], count)

            take_gather(1)
            act.wait_ge(n_ready, 1)
            n = act.value_load(n_t[0:1, 0:1], min_val=PAIRS, max_val=4 * PAIRS)
            with act.Fori(0, n) as it:
                c1 = act.snap(it + 1)
                c2 = act.snap(it + 2)
                c21 = act.snap(2 * it + 1)
                c22 = act.snap(2 * it + 2)

                def copy_gu(e):
                    act.wait_ge(gu_done[e], c1)
                    nc.scalar.activation(gu_sb[:, 0:512], bank[2 * e][:, :], ACT.Copy).then_inc(gu_copied[e][0], 1)

                def sigmoid(count):
                    act.wait_ge(clipped, count)
                    nc.scalar.activation(sg, gu1[:, :, 0, :], ACT.Sigmoid, scale=ALPHA).then_inc(sig_ready, 1)

                copy_gu(0)
                for h in range(2):
                    take(f"S{h}", selgT[:, h * P:h * P + P], TB[h][:, 0:P], c1)
                sigmoid(c21)
                copy_gu(1)
                sigmoid(c22)
                take_gather(c2)
                act.wait_ge(down_done, c1)
                nc.scalar.activation(dsb[:, 0:512], bank[4][:, :], ACT.Copy).then_inc(d_copied[0], 1)

        @block.vector
        def _(dve):
            steps = [0]

            def step(ins):
                steps[0] += 1
                ins.then_inc(dve_step, 1)
                dve.wait_ge(dve_step, steps[0])

            V = nc.vector

            def root_and_reciprocal(col, n, scale, which):
                V.tensor_scalar(small[:, col:col + n], small[:, col:col + n], scale, EPS, ALU.mult, ALU.add).then_inc(ms_ready, 1)
                dve.wait_ge(root_ready, 2 * which - 1)
                V.reciprocal(small[:, col:col + n], small[:, col:col + n]).then_inc(root_ready, 1)
                dve.wait_ge(root_ready, 2 * which)

            def gained(j, c0, b, gain):
                dve.wait_ge(t_ready, j + 1)
                g = cols[:, gain + c0:gain + c0 + 4].unsqueeze(2).to_broadcast([P, 4, P])
                V.tensor_tensor(hT[:, c0:c0 + 4, b * P:b * P + P], v3(TB[j % 2][:, :], 4), g, ALU.mult).then_inc(t_read[j % 2], 1)

            dve.wait_ge(cols_in, 16)
            for j in range(4):
                gained(TJ_X + j, 4 * (j % 2), j // 2, P_G1)
            dve.wait_ge(xn_ready, NB)
            root_and_reciprocal(128, 2, 1.0 / D, 1)
            dve.wait_ge(small_in, 48)
            posf = small[:, 188:190]
            step(V.tensor_copy(posf, posi[:, :]))
            for b in range(NB):
                step(V.tensor_scalar(angs[0][:, 32 * b:32 * b + 32], invf, posf[:, b:b + 1], None, ALU.mult))
            step(V.tensor_scalar(angs[2], angs[0], 1.0 / TWO_PI, None, ALU.mult))
            step(V.tensor_scalar(angs[4], angs[2], MAGIC, None, ALU.add))
            step(V.tensor_scalar(angs[2], angs[4], MAGIC, None, ALU.subtract))
            for part in two_pi_parts():
                step(V.scalar_tensor_tensor(out=angs[0], in0=angs[2], scalar=-part, in1=angs[0], op0=ALU.mult, op1=ALU.add))
            V.tensor_scalar(angs[1], angs[0], 3.1415925, -3.1415925, ALU.min, ALU.max).then_inc(trig_arg, 1)
            step(V.scalar_tensor_tensor(out=angs[4], in0=angs[0], scalar=-1.0, in1=angs[0], op0=ALU.mult, op1=ALU.max))
            V.tensor_scalar(angs[3], angs[4], -1.0, TWO_PI / 4, ALU.mult, ALU.add).then_inc(trig_arg, 1)

            cos = v3(cos_t, NB)
            sin = v3(sin_t, NB)

            def rope(src, outs, nh, half, stride):
                cb = cos[:, :, ::stride].unsqueeze(2).to_broadcast([P, NB, nh, half])
                sb_ = sin[:, :, ::stride].unsqueeze(2).to_broadcast([P, NB, nh, half])
                x1, x2 = src[:, :, :, 0:half], src[:, :, :, half:2 * half]
                t = [r[:, 0:NB * nh * half].rearrange("p (b h n) -> p b h n", b=NB, h=nh) for r in rtmp]
                V.tensor_tensor(t[0], x1, cb, ALU.mult)
                V.tensor_tensor(t[1], x2, sb_, ALU.mult)
                V.tensor_tensor(t[2], x2, cb, ALU.mult)
                step(V.tensor_tensor(t[3], x1, sb_, ALU.mult))
                for o in outs:
                    V.tensor_tensor(o[:, :, :, 0:half], t[0], t[1], ALU.subtract)
                    ins = V.tensor_tensor(o[:, :, :, half:2 * half], t[2], t[3], ALU.add)
                return ins

            def head_squares(src, nh, col):
                sq = big[:, 1024:1024 + NB * nh * HD].rearrange("p (b h n) -> p b h n", b=NB, h=nh)
                step(V.tensor_tensor(sq, src, src, ALU.mult))
                step(V.tensor_reduce(out=small[:, col:col + NB * nh], in_=big[:, 1024:1024 + NB * nh * HD].rearrange("p (a n) -> p a n", n=HD),
                                     op=ALU.add, axis=AX))

            def scaled(src, nh, col, gain):
                r = small[:, col:col + NB * nh].rearrange("p (b h) -> p b h", b=NB).unsqueeze(3).to_broadcast([P, NB, nh, HD])
                g = gain.unsqueeze(1).unsqueeze(1).to_broadcast([P, NB, nh, HD])
                step(V.tensor_tensor(src, src, r, ALU.mult))
                step(V.tensor_tensor(src, src, g, ALU.mult))

            k4 = kvqi[:, :, 0:128].rearrange("p b (h n) -> p b h n", h=KV)
            qi4 = kvqi[:, :, 256:512].rearrange("p b (h n) -> p b h n", h=IH)
            q4 = qq.rearrange("p b (h n) -> p b h n", h=HEADS)
            ki3 = kiwi[:, :, 0:64]
            wi3 = kiwi[:, :, 64:68]
            dve.wait_ge(job_read, 2)
            head_squares(k4, KV, 132)
            dve.wait_ge(job_read, 4)
            step(V.tensor_reduce(out=small[:, 192:194], in_=ki3, op=ALU.add, axis=AX))
            step(V.tensor_scalar(small[:, 192:194], small[:, 192:194], -1.0 / ID, None, ALU.mult))
            step(V.tensor_tensor(ki3, ki3, small[:, 192:194].unsqueeze(2).to_broadcast([P, NB, ID]), ALU.add))
            step(V.tensor_tensor(v3(rtmp[3][:, 0:NB * ID], NB), ki3, ki3, ALU.mult))
            step(V.tensor_reduce(out=small[:, 136:138], in_=v3(rtmp[3][:, 0:NB * ID], NB), op=ALU.add, axis=AX))
            root_and_reciprocal(132, 6, 1.0 / HD, 2)
            scaled(k4, KV, 132, rows[:, R_KG:R_KG + HD])
            dve.wait_ge(trig_ready, 2)
            rope(k4, [kdup[:, :, :, 0:64], kdup[:, :, :, 64:128]], KV, 32, 1).then_inc(roped, 1)
            dve.wait_ge(roped, 1)
            step(V.tensor_tensor(ki3, ki3, small[:, 136:138].unsqueeze(2).to_broadcast([P, NB, ID]), ALU.mult))
            step(V.tensor_tensor(ki3, ki3, rows[:, R_IG:R_IG + ID].unsqueeze(1).to_broadcast([P, NB, ID]), ALU.mult))
            step(V.tensor_tensor(ki3, ki3, rows[:, R_IB:R_IB + ID].unsqueeze(1).to_broadcast([P, NB, ID]), ALU.add))
            kd4 = kidup.rearrange("p b (r n) -> p b r n", r=2)
            rope(ki3.unsqueeze(2), [kd4[:, :, 0:1, :], kd4[:, :, 1:2, :]], 1, 16, 2)
            V.tensor_copy(kd4[:, :, 0, IROPE:], ki3[:, :, IROPE:])
            V.tensor_copy(kd4[:, :, 1, IROPE:], ki3[:, :, IROPE:]).then_inc(roped, 1)
            dve.wait_ge(roped, 2)
            rope(qi4, [qi4], IH, 16, 2).then_inc(roped, 1)
            dve.wait_ge(roped, 3)
            step(V.tensor_scalar(wi3, wi3, IDX_SCALE, None, ALU.mult))
            dve.wait_ge(job_read, 6)
            head_squares(q4, HEADS, 140)
            root_and_reciprocal(140, 16, 1.0 / HD, 3)
            scaled(q4, HEADS, 140, rows[:, R_QG:R_QG + HD])
            rope(q4, [q4], HEADS, 32, 1).then_inc(roped, 1)
            dve.wait_ge(roped, 4)
            for b in range(NB):
                nk = P * (b + 1)
                short_read(dve, (TJ_L0, TJ_L1)[b] + 2)
                step(V.tensor_scalar(score[:, b, 0:nk], relu[:, 0, 0:nk], wi3[:, b, 0:1], None, ALU.mult))
                for h in range(1, IH):
                    ins = V.scalar_tensor_tensor(out=score[:, b, 0:nk], in0=relu[:, h, 0:nk], scalar=wi3[:, b, h:h + 1],
                                                 in1=score[:, b, 0:nk], op0=ALU.mult, op1=ALU.add)
                    if h < IH - 1:
                        step(ins)
                ins.then_inc(relu_used, 1)
                dve.wait_ge(relu_used, b + 1)
                step(V.memset(score[0:CHUNK, b, nk - CHUNK:nk], NEG_MASK))
                top = small[:, 196:204]
                src = score[:, b, 0:nk]
                for r in range(N_SEL // 8):
                    step(V.max(out=top, in_=src))
                    step(V.match_replace(out=work[:, b, 0:nk], in_to_replace=top, in_values=src, imm_value=REPL))
                    src = work[:, b, 0:nk]
                step(V.tensor_scalar(pen[:, b, 0:nk], work[:, b, 0:nk], -3.395e38, -1.0e30, ALU.is_gt, ALU.mult))
            for b in range(NB):
                nk = P * (b + 1)
                per = BANK // nk
                first = TJ_S0 if b == 0 else TJ_S1
                if b == 1:
                    dve.wait_ge(t_ready, TJ_X + 4)
                for j in range(HEADS // per):
                    dve.wait_ge(t_ready, first + j + 1)
                    h0 = 4 * (j // 2) + j % 2 if b == 1 else j
                    V.scalar_tensor_tensor(out=att[b][:, h0:h0 + 2 * per - 1:2, :], in0=v3(TB[(first + j) % 2][:, :], per),
                                           scalar=SCALE, in1=pen[:, b, 0:nk].unsqueeze(1).to_broadcast([P, per, nk]),
                                           op0=ALU.mult, op1=ALU.add).then_inc(t_read[(first + j) % 2], 1)
                short_read(dve, first + HEADS // per)
                mx = small[:, 156 + 8 * b:164 + 8 * b]
                step(V.tensor_reduce(out=mx, in_=att[b], op=ALU.max, axis=AX))
                V.tensor_scalar(mx, mx, -1.0, None, ALU.mult).then_inc(att_masked, 1)
            for b in range(NB):
                nk = P * (b + 1)
                sums = small[:, 172 + 8 * b:180 + 8 * b]
                dve.wait_ge(att_exp, 8 * (b + 1))
                step(V.reciprocal(sums, sums))
                V.tensor_tensor(att[b], att[b], sums.unsqueeze(2).to_broadcast([P, HEADS, nk]), ALU.mult).then_inc(prob_ready, 1)

            def tcopy(j, dst):
                dve.wait_ge(t_ready, j + 1)
                V.tensor_copy(dst, v3(TB[j % 2][:, :], 4)).then_inc(t_read[j % 2], 1)

            tcopy(TJ_P0 + 1, PT[0][:, 0, 4:8, :])
            tcopy(TJ_P1 + 1, PT[1][:, 0, 4:8, :])
            tcopy(TJ_P1 + 3, PT[1][:, 1, 4:8, :])
            for j in range(2):
                dve.wait_ge(t_ready, TJ_POOL + j + 1)
                V.tensor_tensor(pooledT[:, 2 * j:2 * j + 2, :], v3(TB[(TJ_POOL + j) % 2][:, :], 2),
                                cols[:, P_PS + 2 * j:P_PS + 2 * j + 2].unsqueeze(2).to_broadcast([P, 2, SEQ]),
                                ALU.mult).then_inc(t_read[(TJ_POOL + j) % 2], 1)
            dve.wait_ge(job_read, 16)

            def gated(j0, b, gate):
                j = j0 + b
                for h in range(2):
                    dve.wait_ge(job_ready, 2 * j + 1 + h)
                    V.tensor_tensor(gate[:, b, 512 * h:512 * h + 512], bank[PAIR_BANKS[j % 3][h]][:, :],
                                    gate[:, b, 512 * h:512 * h + 512], ALU.mult).then_inc(job_read, 1)

            for b in range(NB):
                gated(BJ_WA, b, siga)
            for b in range(NB):
                gated(BJ_WB, b, sigp)
                dve.wait_ge(job_read, 2 * (BJ_WB + b) + 2)
                V.tensor_tensor(siga[:, b, :], siga[:, b, :], sigp[:, b, :], ALU.add).then_inc(merged_ready, 1)
            for j in (1, 3):
                tcopy(TJ_M + j, hT[:, 4:8, (j // 2) * P:(j // 2) * P + P])
            for b in range(NB):
                j = BJ_WO + b
                for h in range(2):
                    dve.wait_ge(job_ready, 2 * j + 1 + h)
                    V.tensor_tensor(x[:, b, 512 * h:512 * h + 512], bank[PAIR_BANKS[j % 3][h]][:, :],
                                    x[:, b, 512 * h:512 * h + 512], ALU.add).then_inc(job_read, 1)
                dve.wait_ge(job_read, 2 * j + 2)
                dve.sem_inc(x2_ready, 1)
                if b == 0:
                    for g in range(2):
                        gained(TJ_H2[0] + g, 4 * g, 0, P_G2)
            for g in range(2):
                gained(TJ_H2[1] + g, 4 * g, 1, P_G2)
            dve.wait_ge(xn_ready, 2 * NB)
            root_and_reciprocal(128, 2, 1.0 / D, 4)
            lgp = v3(rt_t[:, 0:80], NB)
            rex = v3(rt_t[:, 128:192], NB)
            rwork = v3(rt_t[:, 512:592], NB)
            msk = v3(rt_t[:, 640:704], NB)
            gex = v3(rt_t[:, 704:768], NB)
            step(V.memset(lgp[:, :, E:E + 8], PAD))
            tops = small[:, 204:220]
            for b in range(NB):
                j = TJ_R[b]
                dve.wait_ge(t_ready, j + 1)
                V.scalar_tensor_tensor(out=lgp[:, b, 0:E], in0=TB[j % 2][:, 0:E], scalar=small[:, 128 + b:129 + b],
                                       in1=rows[:, R_RB:R_RB + E], op0=ALU.mult, op1=ALU.add).then_inc(t_read[j % 2], 1)
                dve.wait_ge(t_read[j % 2], j // 2 + 1)
                step(V.max(out=tops[:, 8 * b:8 * b + 8], in_=lgp[:, b, 0:E]))
                step(V.memset(tops[:, 8 * b + TOPK:8 * b + 8], PAD))
            V.tensor_scalar(small[:, 190:192], v3(tops, NB)[:, :, 0], -1.0, None, ALU.mult).then_inc(lg_ready, 1)
            for b in range(NB):
                step(V.match_replace(out=rwork[:, b, :], in_to_replace=tops[:, 8 * b:8 * b + 8], in_values=lgp[:, b, :], imm_value=REPL))
            V.tensor_scalar(msk, rwork[:, :, 0:E], -3.395e38, None, ALU.is_lt).then_inc(chosen_ready, 1)
            dve.wait_ge(chosen_ready, 1)
            dve.wait_ge(ex_ready, 2)
            step(V.tensor_tensor(gex, rex, msk, ALU.mult))
            step(V.tensor_reduce(out=small[:, 220:222], in_=gex, op=ALU.add, axis=AX))
            step(V.reciprocal(small[:, 220:222], small[:, 220:222]))
            V.tensor_tensor(gat, gex, small[:, 220:222].unsqueeze(2).to_broadcast([P, NB, E]), ALU.mult).then_inc(gates_ready, 1)
            notm = v3(rt_t[:, 768:832], NB)
            step(V.tensor_scalar(notm, msk, -BIG_RANK, BIG_RANK, ALU.mult, ALU.add))
            dve.wait_ge(t_ready, TJ_RANK + 1)
            ranks = v3(TB[TJ_RANK % 2][:, 0:SEQ], NB)[:, :, 0:E]
            step(V.tensor_tensor(rank, ranks, notm, ALU.add))
            iota4 = iota.unsqueeze(1).unsqueeze(1).to_broadcast([P, NB, 2, T])

            def make_sel(p):
                r = rank[:, :, bass.ds(2 * p, 2)].unsqueeze(3).to_broadcast([P, NB, 2, T])
                V.tensor_tensor(sel, iota4, r, ALU.is_equal).then_inc(sel_ready, 1)

            make_sel(0)
            V.tensor_reduce(out=small[:, 222:223], in_=TB[TJ_RANK % 2][:, SEQ:SEQ + E], op=ALU.max, axis=AX).then_inc(t_read[TJ_RANK % 2], 1)
            dve.wait_ge(t_read[TJ_RANK % 2], TJ_RANK // 2 + 1)
            cnt = small[:, 222:223]
            step(V.tensor_scalar(small[:, 223:224], cnt, float(T), None, ALU.is_gt))
            for r in (2, 3):
                step(V.scalar_tensor_tensor(out=small[:, 223:224], in0=cnt, scalar=float(r * T), in1=small[:, 223:224], op0=ALU.is_gt, op1=ALU.add))
            V.tensor_scalar(n_t[:, :], small[:, 223:224], float(PAIRS), float(PAIRS), ALU.mult, ALU.add).then_inc(n_ready, 1)
            dve.wait_ge(n_ready, 1)
            def take_xgT(count):
                for h in range(2):
                    dve.wait_ge(done[f"X{h}"], count)
                    g = cols[:, P_G2 + 4 * h:P_G2 + 4 * h + 4].unsqueeze(2).to_broadcast([P, 4, P])
                    V.tensor_tensor(xgT[:, 4 * h:4 * h + 4, :], v3(TB[h][:, :], 4), g, ALU.mult).then_inc(read[f"X{h}"], 1)

            def add_bias(b, banks, freed):
                for h in range(2):
                    dve.wait_ge(bd_ready, 2 * b + h + 1)
                    V.tensor_tensor(x[:, b, 512 * h:512 * h + 512], banks[h][:, :],
                                    x[:, b, 512 * h:512 * h + 512], ALU.add).then_inc(freed[h], 1)

            take_xgT(1)
            add_bias(0, bank[4:6], d_copied)
            add_bias(1, bank[2:4], gu_copied[1])
            for h in range(2):
                dve.wait_ge(d_copied[h], 1)
                dve.wait_ge(gu_copied[1][h], 1)
            n = dve.value_load(n_t[0:1, 0:1], min_val=PAIRS, max_val=4 * PAIRS)
            with dve.Fori(0, n) as it:
                c1 = dve.snap(it + 1)
                c2 = dve.snap(it + 2)
                here = dve.snap(it % PAIRS)
                after = dve.snap((it + 1) % PAIRS)
                dve.wait_ge(sel_ready, c1)
                dve.wait_ge(read["Y3"], c1)
                g = gat[:, :, bass.ds(2 * here, 2)].unsqueeze(3).to_broadcast([P, NB, 2, T])
                V.tensor_tensor(selg, sel, g, ALU.mult).then_inc(selg_ready, 1)
                rk = rank[:, :, bass.ds(2 * here, 2)]
                V.tensor_scalar(rk, rk, float(T), None, ALU.subtract).then_inc(rank_down, 1)
                dve.wait_ge(selg_ready, c1)
                dve.wait_ge(rank_down, c1)
                dve.wait_ge(done["G1"], c1)
                make_sel(after)

                def swiglu(e):
                    name = "AB"[e]
                    cnt = dve.snap(2 * it + 1 + e)
                    dve.wait_ge(gu_done[e], c1)
                    V.tensor_copy(gu_sb[:, 512:1024], bank[2 * e + 1][:, :]).then_inc(gu_copied[e][1], 1)
                    if e == 1:
                        dve.wait_ge(act_ready, dve.snap(2 * it + 2))
                    for h in range(2):
                        j = f"T{name}{h}"
                        dve.wait_ge(done[j], c1)
                        bias = bgu[:, bass.ds(2 * here + e, 1), 4 * h:4 * h + 4, :].rearrange("p e c g -> p (e c) g")
                        V.tensor_tensor(gu1[:, 4 * h:4 * h + 4, :, :], v4(TB[h][:, :], 4, 2),
                                        bias.unsqueeze(3).to_broadcast([P, 4, 2, T]), ALU.add).then_inc(read[j], 1)
                    for h in range(2):
                        dve.wait_ge(read[f"T{name}{h}"], c1)
                    V.tensor_scalar(gu1[:, :, 0, :], gu1[:, :, 0, :], LIMIT, None, ALU.min).then_inc(clipped, 1)
                    V.tensor_scalar(up1, gu1[:, :, 1, :], LIMIT, -LIMIT, ALU.min, ALU.max).then_inc(up_ready, 1)
                    dve.wait_ge(clipped, cnt)
                    dve.wait_ge(up_ready, cnt)
                    V.scalar_tensor_tensor(out=up1, in0=up1, scalar=1.0, in1=gu1[:, :, 0, :],
                                           op0=ALU.add, op1=ALU.mult).then_inc(prod_ready, 1)
                    dve.wait_ge(prod_ready, cnt)
                    dve.wait_ge(sig_ready, cnt)
                    V.tensor_tensor(actT[:, :, T * e:T * e + T], up1, sg, ALU.mult).then_inc(act_ready, 1)

                swiglu(0)
                swiglu(1)
                take_xgT(c2)
                dve.wait_ge(down_done, c1)
                V.tensor_copy(dsb[:, 512:1024], bank[5][:, :]).then_inc(d_copied[1], 1)
                for j in range(4):
                    b, h = j // 2, j % 2
                    dve.wait_ge(done[f"Y{j}"], c1)
                    V.tensor_tensor(x[:, b, 512 * h:512 * h + 512], TB[h][:, :], x[:, b, 512 * h:512 * h + 512],
                                    ALU.add).then_inc(read[f"Y{j}"], 1)

        @block.tensor
        def _(pe):
            MM = nc.tensor.matmul
            for s in range(RING, SLOTS):
                pe.sem_inc(unit_used[s], PRE_TURNS)
            tj = [0]

            def t_job(j):
                assert j == tj[0], (j, tj[0])
                tj[0] += 1
                if j >= 2:
                    pe.wait_ge(t_read[j % 2], j // 2)
                return TB[j % 2]

            def transposes(j, srcs):
                dst = t_job(j)
                for k, s in enumerate(srcs):
                    ins = nc.tensor.transpose(dst[:, k * P:k * P + P], s, ident)
                ins.then_inc(t_ready, 1)

            def unit(u):
                s = u % RING
                pe.wait_ge(unit_in[s], 16 * (u // RING + 1))
                return ring[s]

            def free_unit(u, ins):
                ins.then_inc(unit_used[u % RING], 1)

            def free_banks(j):
                if j >= 3:
                    pe.wait_ge(job_read, 2 * (j - 2))

            def projection(j):
                free_banks(j)
                n = groups[j][1]
                for half in range(2):
                    u = 2 * j + half
                    w = v3(unit(u)[:, 0:4 * n], 4)
                    for b in range(NB):
                        for k in range(4):
                            kc = 4 * half + k
                            ins = MM(bank[PAIR_BANKS[j % 3][b]][:, 0:n], hT[:, kc, b * P:b * P + P], w[:, k, :],
                                     start=kc == 0, stop=kc == KC - 1)
                        if half == 0 and b == 1:
                            free_unit(u, ins)
                        if half == 1:
                            ins.then_inc(job_ready, 1)
                    if half == 1:
                        pe.wait_ge(job_ready, 2 * j + 2)
                        pe.sem_inc(unit_used[u % RING], 1)

            def branch(b, j0, u0, nk, lhs, between=None):
                j = j0 + b
                free_banks(j)
                for k in range(nk):
                    if between is not None and k == nk // 2:
                        between()
                    u = u0 + k // 2
                    w = v3(unit(u)[:, :], 2)
                    for h in range(2):
                        ins = MM(bank[PAIR_BANKS[j % 3][h]][:, :], lhs[:, k, b * P:b * P + P], w[:, k % 2, 512 * h:512 * h + 512],
                                 start=k == 0, stop=k == nk - 1)
                        if k == nk - 1:
                            ins.then_inc(job_ready, 1)
                    if b == NB - 1 and k % 2 == 1 and k < nk - 1:
                        free_unit(u, ins)
                if b == NB - 1:
                    pe.wait_ge(job_ready, 2 * (j0 + NB))
                    pe.sem_inc(unit_used[(u0 + nk // 2 - 1) % RING], 1)

            pe.wait_ge(ident_in, 16)
            for b in range(NB):
                pe.wait_ge(x_in[b], 16)
                for g in range(2):
                    transposes(TJ_X + 2 * b + g, [x[:, b, (4 * g + k) * P:(4 * g + k + 1) * P] for k in range(4)])
            short_read(pe, TJ_X + 4)
            for j in range(4):
                projection(j)
            pe.wait_ge(roped, 1)
            transposes(TJ_K, [kdup[:, b, kv, :] for b in range(NB) for kv in range(KV)])
            pe.wait_ge(roped, 3)
            transposes(TJ_QI, [kvqi[:, b, 256 + P * g:256 + P * g + P] for b in range(NB) for g in range(2)])
            transposes(TJ_KI, [kidup[:, b, :] for b in range(NB)])
            short_read(pe, TJ_KI + 1)
            for b in range(NB):
                nk = P * (b + 1)
                for par in range(2):
                    dst = t_job((TJ_L0, TJ_L1)[b] + par)
                    for i in range(2):
                        h = 2 * i + par
                        r = 64 * (h % 2)
                        ins = MM(dst[:, i * nk:i * nk + nk], qiT[r:r + 64, h // 2, b * P:b * P + P], kiT_t[r:r + 64, 0:nk],
                                 start=True, stop=True)
                    ins.then_inc(t_ready, 1)
            projection(4)
            pe.wait_ge(roped, 4)
            for b in range(NB):
                transposes(TJ_Q + b, [qq[:, b, P * g:P * g + P] for g in range(4)])
            projection(5)
            short_read(pe, TJ_Q + 2)
            for b in range(NB):
                nk = P * (b + 1)
                per = BANK // nk
                for g in range(HEADS // per):
                    dst = t_job((TJ_S0 if b == 0 else TJ_S1) + g)
                    h0 = 4 * (g // 2) + g % 2 if b == 1 else g
                    for i in range(per):
                        h = h0 + 2 * i
                        r = 64 * (h % 2)
                        ins = MM(dst[:, i * nk:i * nk + nk], qT[r:r + 64, h // 2, b * P:b * P + P], kT[r:r + 64, h // 4, 0:nk],
                                 start=True, stop=True)
                    ins.then_inc(t_ready, 1)
            projection(6)
            for b in range(NB):
                pe.wait_ge(prob_ready, b + 1)
                for kb in range(b + 1):
                    for g in range(2):
                        transposes((TJ_P0 if b == 0 else TJ_P1) + 2 * kb + g,
                                   [att[b][:, 4 * g + i, kb * P:kb * P + P] for i in range(4)])
            projection(7)
            pe.wait_ge(late_in, 48)
            pe.wait_ge(job_read, 8)
            for j in range(2):
                dst = t_job(TJ_MIX + j)
                for i in range(2):
                    g = 2 * j + i
                    MM(dst[:, i * SEQ:i * SEQ + P], pool[:, 0, g * P:g * P + P], bands[:, g, 0, :], start=True, stop=True)
                    MM(dst[:, i * SEQ + P:(i + 1) * SEQ], pool[:, 0, g * P:g * P + P], bands[:, g, 1, :], start=True, stop=False)
                    ins = MM(dst[:, i * SEQ + P:(i + 1) * SEQ], pool[:, 1, g * P:g * P + P], bands[:, g, 2, :], start=False, stop=True)
                ins.then_inc(t_ready, 1)
            for b in range(NB):
                dst = t_job(TJ_O + b)
                for kv in range(KV):
                    for par in range(2):
                        for kb in range(b + 1):
                            h0 = 4 * kv + par
                            ins = MM(dst[64 * par:64 * par + 64, kv * 2 * P:(kv + 1) * 2 * P],
                                     kvqi[:, kb, P + 64 * kv:P + 64 * kv + 64], PT[b][:, kb, h0:h0 + 3:2, :],
                                     start=kb == 0, stop=kb == b)
                ins.then_inc(t_ready, 1)
            for j in range(2):
                dst = t_job(TJ_POOL + j)
                for i in range(2):
                    g = 2 * j + i
                    ins = MM(dst[:, i * SEQ:(i + 1) * SEQ], mixw[:, g, :], mixedT[:, g, :], start=True, stop=True)
                ins.then_inc(t_ready, 1)
            for b in range(NB):
                branch(b, BJ_WA, 16, 4, attnT)
            short_read(pe, TJ_POOL + 2)
            for b in range(NB):
                branch(b, BJ_WB, 18, 4, pooledT)

            def turn_merged(b):
                pe.wait_ge(merged_ready, b + 1)
                for g in range(2):
                    transposes(TJ_M + 2 * b + g, [siga[:, b, (4 * g + k) * P:(4 * g + k + 1) * P] for k in range(4)])

            def turn_x2(b):
                pe.wait_ge(x2_ready, b + 1)
                for g in range(2):
                    transposes(TJ_H2[b] + g, [x[:, b, (4 * g + k) * P:(4 * g + k + 1) * P] for k in range(4)])

            turn_merged(0)
            short_read(pe, TJ_M + 2)
            branch(0, BJ_WO, 20, 8, hT, lambda: turn_merged(1))
            short_read(pe, TJ_M + 4)
            branch(1, BJ_WO, 20, 8, hT, lambda: turn_x2(0))
            pe.wait_ge(rw_in, 16)
            turn_x2(1)
            for b in range(NB):
                dst = t_job(TJ_R[b])
                short_read(pe, TJ_H2[b] + 2)
                for k in range(KC):
                    ins = MM(dst[:, 0:E], hT[:, k, b * P:b * P + P], rw[:, k, :], start=k == 0, stop=k == KC - 1)
                ins.then_inc(t_ready, 1)
            pe.wait_ge(chosen_ready, 1)
            dst = t_job(TJ_RANK)
            msk = v3(rt_t[:, 640:704], NB)
            MM(dst[:, 0:E], tri, msk[:, 0, :], start=True, stop=True)
            MM(dst[:, P:P + E], ones, msk[:, 0, :], start=True, stop=False)
            MM(dst[:, P:P + E], tri, msk[:, 1, :], start=False, stop=True)
            MM(dst[:, SEQ:SEQ + E], ones, msk[:, 0, :], start=True, stop=False)
            MM(dst[:, SEQ:SEQ + E], ones, msk[:, 1, :], start=False, stop=True).then_inc(t_ready, 1)
            pe.wait_ge(job_read, 2 * (BJ_WO + NB))
            pe.wait_ge(gates_ready, 1)
            for b in range(NB):
                MM(bank[0][0:E, b * P:b * P + P], gat[:, b, :], ident, start=True, stop=True).then_inc(gatesT_ready, 1)
            short_read(pe, TJ_RANK + 1)
            pe.wait_ge(xn_ready, 3 * NB)

            def gather(count):
                pe.wait_ge(sel_ready, count)
                for h in range(2):
                    for b in range(NB):
                        ins = MM(TB[h][:, :], selb[:, b * P:b * P + P], xn[:, b, 512 * h:512 * h + 512], start=b == 0, stop=b == NB - 1)
                    ins.then_inc(done[f"G{h}"], 1)

            def turn(name, src, h):
                for k in range(4):
                    c = 4 * h + k
                    ins = nc.tensor.transpose(TB[h][:, k * P:k * P + P], src[:, c * P:c * P + P], ident)
                ins.then_inc(done[f"{name}{h}"], 1)

            def bias(j):
                b, h = j // 2, j % 2
                MM(bank[4 - 2 * b + h][:, :], rt_t[0:E, 256 + b * P:256 + b * P + P], bd_sb[:, 512 * h:512 * h + 512],
                   start=True, stop=True).then_inc(bd_ready, 1)

            def pair_step(count, it, half, turns, turns_in, with_bias):
                c1 = count(2 * it + (half + 1))
                c2 = count(2 * it + (half + 2))
                a3 = count(4 * it + (2 * half + 3))

                def landed(u):
                    t, s = divmod(PAIR_UNITS * half + u, SLOTS)
                    pe.wait_ge(unit_in[s], turns_in[t])
                    return s

                def all_used(u):
                    t, s = divmod(PAIR_UNITS * half + u, SLOTS)
                    pe.wait_ge(unit_used[s], turns[t])

                def gate_up(e, k):
                    s = landed(8 * e + k)
                    for h in range(2):
                        for g in range(2):
                            ins = MM(bank[2 * e + h][T * g:T * g + T, :], xgT[:, k, T * e:T * e + T],
                                     ring[s][:, D * g + 512 * h:D * g + 512 * h + 512], start=k == 0, stop=k == KC - 1)
                    ins.then_inc(unit_used[s], 1)

                for h in range(2):
                    pe.wait_ge(gu_copied[0][h], c1)
                for k in range(KC):
                    if k % 4 == 0:
                        pe.wait_ge(read[f"X{k // 4}"], c1)
                    gate_up(0, k)
                    if with_bias and 3 <= k < 7:
                        bias(k - 3)
                all_used(7)
                pe.sem_inc(gu_done[0], 1)
                for h in range(2):
                    pe.wait_ge(gu_copied[1][h], c1)
                for k in range(2):
                    gate_up(1, k)
                for h in range(2):
                    pe.wait_ge(read[f"Y{2 + h}"], c1)
                    pe.wait_ge(gu_copied[0][h], c2)
                    turn("TA", gu_sb, h)
                pe.wait_ge(selg_ready, c1)
                for b in range(NB):
                    pe.wait_ge(read[f"TA{b}"], c1)
                    nc.tensor.transpose(TB[b][:, 0:P], selgb[:, b * P:b * P + P], ident).then_inc(done[f"S{b}"], 1)
                for k in range(2, KC):
                    gate_up(1, k)
                all_used(15)
                pe.sem_inc(gu_done[1], 1)
                for h in range(2):
                    pe.wait_ge(read[f"S{h}"], c1)
                    pe.wait_ge(gu_copied[1][h], c2)
                    turn("TB", gu_sb, h)
                for h in range(2):
                    pe.wait_ge(read[f"TB{h}"], c1)
                gather(c2)
                for h in range(2):
                    pe.wait_ge(read[f"G{h}"], c2)
                for h in range(2):
                    turn("X", xg, h)
                pe.wait_ge(act_ready, a3)
                pe.wait_ge(d_copied[0], c1)
                pe.wait_ge(d_copied[1], c1)
                for k2 in range(KC // 2):
                    ws = []
                    for e in range(2):
                        ws.append(landed(16 + 2 * k2 + e))
                    for k in range(2):
                        c = 2 * k2 + k
                        for h in range(2):
                            for e in range(2):
                                ins = MM(bank[4 + h][T * e:T * e + T, :], actT[:, c, T * e:T * e + T],
                                         v3(ring[ws[e]][:, :], 2)[:, k, 512 * h:512 * h + 512], start=c == 0, stop=c == KC - 1)
                                if k == 1 and h == 1:
                                    ins.then_inc(unit_used[ws[e]], 1)
                all_used(23)
                pe.sem_inc(down_done, 1)
                pe.wait_ge(d_copied[0], c2)
                pe.wait_ge(d_copied[1], c2)
                for j in range(4):
                    b, h = j // 2, j % 2
                    if b == 0:
                        pe.wait_ge(read[f"X{h}"], c2)
                    else:
                        pe.wait_ge(read[f"Y{h}"], c2)
                    MM(TB[h][:, :], selgT[:, b * P:b * P + P], dsb[:, 512 * h:512 * h + 512],
                       start=True, stop=True).then_inc(done[f"Y{j}"], 1)

            gather(1)
            for h in range(2):
                pe.wait_ge(read[f"G{h}"], 1)
                turn("X", xg, h)
            pe.wait_ge(gatesT_read, 1)
            pe.wait_ge(bd_in, 16)
            pe.wait_ge(n_ready, 1)
            n = pe.value_load(n_t[0:1, 0:1], min_val=PAIRS, max_val=4 * PAIRS)
            n2 = pe.snap(n // 2)

            def two_pairs(count, it, with_bias):
                turns = [count(3 * it + (t + 1 + PRE_TURNS)) for t in range(3)]
                turns_in = [count(48 * it + 16 * (t + 1 + PRE_TURNS)) for t in range(3)]
                for half in range(2):
                    pair_step(count, it, half, turns, turns_in, with_bias and half == 0)

            two_pairs(int, 0, True)
            with pe.Fori(1, n2) as it:
                two_pairs(pe.snap, it, False)


def constant_tables():
    import numpy as np
    t = np.zeros((P, K_W), np.float32)
    t[:, K_IDENT:K_IDENT + P] = np.eye(P)
    t[:, K_TRI:K_TRI + P] = np.triu(np.ones((P, P)), 1)
    t[:, K_ONES:K_ONES + P] = 1.0
    t[:, K_IOTA:K_IOTA + T] = np.arange(T)
    t[:, K_INVF:K_INVF + 32] = np.power(np.float32(10000.0), -(np.arange(0, HD, 2, dtype=np.float32) / np.float32(HD)))
    bands = np.zeros((GROUPS, SEQ, SEQ), np.float32)
    for g, w in enumerate(WINDOWS):
        for s in range(SEQ):
            lo = max(s + 1 - w, 0)
            bands[g, lo:s + 1, s] = 1.0 / (s + 1 - lo)
            bands[g, s, s] -= 1.0
    b = np.stack([bands[:, :P, :P], bands[:, :P, P:], bands[:, P:, P:]], axis=1)
    return t, np.ascontiguousarray(b.transpose(2, 0, 1, 3).reshape(P, GROUPS * 3 * P))


def kernel(**inputs):
    import numpy as np
    import concourse.bacc as bacc
    from concourse import mybir as mb
    from concourse.bass_utils import run_bass_kernel_spmd

    a = {k: np.ascontiguousarray(v) for k, v in inputs.items()}
    consts, bands = constant_tables()
    rows = np.concatenate([a[k].reshape(-1) for k in ("q_norm_g", "k_norm_g", "idx_k_norm_g", "idx_k_norm_b", "router_b")])
    cols = np.concatenate([a["norm1_g"].reshape(KC, P).T, a["pool_scale"].reshape(GROUPS, P).T,
                           a["norm2_g"].reshape(KC, P).T], axis=1)
    bgu = a["b_gate_up"].reshape(E, 2, KC, P).transpose(3, 0, 2, 1).reshape(P, E * KC * 2)
    arrays = {
        "x": a["x"].reshape(SEQ, D), "positions": a["positions"].reshape(NB, P).T, "w_in": a["w_in"].reshape(D, IN_W),
        "w_branch_attn": a["w_branch_attn"].reshape(512, D), "w_branch_pool": a["w_branch_pool"].reshape(512, D),
        "w_out": a["w_out"].reshape(D, D), "pool_mix_w": a["pool_mix_w"].reshape(GROUPS, P, P),
        "router_w": a["router_w"].reshape(D, E), "w_gate_up": a["w_gate_up"].reshape(E * D, 2 * D),
        "w_down": a["w_down"].reshape(E * D, D), "b_down": a["b_down"].reshape(E, D),
        "consts": consts, "bands": bands, "rows": rows.reshape(1, R_W), "cols": cols, "bgu": bgu,
    }
    arrays = {f"{k}_dram": np.ascontiguousarray(v) for k, v in arrays.items()}
    nc = bacc.Bacc("TRN2", target_bir_lowering=False, num_devices=1)
    args = [nc.dram_tensor(k, v.shape, mb.dt.from_np(v.dtype), kind="ExternalInput").ap() for k, v in arrays.items()]
    out = nc.dram_tensor("out_dram", (SEQ, D), mb.dt.float32, kind="ExternalOutput").ap()
    block_kernel(nc, *args, out)
    r = run_bass_kernel_spmd(nc, [arrays], core_ids=[0])
    return r.results[0]["out_dram"].reshape(1, SEQ, D)
```
